# Optimizing a Trainium2 kernel written in Bass

```python
import math
import jax
import jax.numpy as jnp
from jax import lax
import numpy as np

D_MODEL = 1024
BATCH = 1
SEQ = 256
DEPTH = 2

MEM_LEN = 256
EPS = 1e-6

N_Q_HEADS = 16
N_KV_HEADS = 2
HEAD_DIM = 64
WINDOW = 128
BLOCK = 128
N_BUCKETS = 32
MAX_DISTANCE = 128
N_X_HEADS = 4
X_HEAD_DIM = 256
EXPAND = 2
D_INNER = EXPAND * D_MODEL
SSM_HEAD_DIM = 64
N_SSM_HEADS = D_INNER // SSM_HEAD_DIM
N_SSM_GROUPS = 4
HEADS_PER_GROUP = N_SSM_HEADS // N_SSM_GROUPS
D_STATE = 128
CONV_WIDTH = 4
CHUNK = 128
DT_MIN = 1e-3
DT_MAX = 1e-1
D_FF = 2816
N_EXPERTS = 8
TOP_K = 2

Q_W = N_Q_HEADS * HEAD_DIM
KV_W = N_KV_HEADS * HEAD_DIM
XQ_W = N_X_HEADS * X_HEAD_DIM
SWA_IN_W = Q_W + 2 * KV_W + XQ_W
SWA_CAT_W = Q_W + XQ_W
BC_W = N_SSM_GROUPS * D_STATE
CONV_CH = D_INNER + 2 * BC_W
SSM_IN_W = D_INNER + CONV_CH + N_SSM_HEADS + XQ_W
SSM_CAT_W = D_INNER + XQ_W
N_EVEN = (DEPTH + 1) // 2
N_ODD = DEPTH // 2

kernel_name = 'hybrid_swa_ssd_moe_memory_trunk'

def rmsnorm(x, g):
    xf = x.astype(jnp.float32)
    y = xf * lax.rsqrt(jnp.mean(xf * xf, axis=-1, keepdims=True) + EPS)
    return (y * g.astype(jnp.float32)).astype(x.dtype)

def t5_bucket(dist):
    max_exact = N_BUCKETS // 2
    d = jnp.maximum(dist, 0)
    df = jnp.maximum(d, 1).astype(jnp.float32)
    far = max_exact + (jnp.log(df / max_exact) / math.log(MAX_DISTANCE / max_exact) * (N_BUCKETS - max_exact)).astype(jnp.int32)
    return jnp.where(d < max_exact, d, jnp.minimum(far, N_BUCKETS - 1))

def sliding_window_attention(q, k, v, sinks, rel_bias):
    b, s = q.shape[0], q.shape[1]
    nb = s // BLOCK
    grp = N_Q_HEADS // N_KV_HEADS
    qb = q.reshape(b, nb, BLOCK, N_KV_HEADS, grp, HEAD_DIM).transpose(1, 0, 3, 4, 2, 5)

    def band_keys(t):
        tb = t.reshape(b, nb, BLOCK, N_KV_HEADS, HEAD_DIM)
        prev = jnp.concatenate([jnp.zeros_like(tb[:, :1]), tb[:, :-1]], axis=1)
        return jnp.concatenate([prev, tb], axis=2).transpose(1, 0, 3, 2, 4)

    kw, vw = band_keys(k), band_keys(v)
    qi = jnp.arange(BLOCK)[:, None]
    kj = jnp.arange(2 * BLOCK)[None, :]
    dist = BLOCK + qi - kj
    band = (dist >= 0) & (dist < WINDOW)
    bias = rel_bias[t5_bucket(dist)].astype(jnp.float32).transpose(2, 0, 1).reshape(N_KV_HEADS, grp, BLOCK, 2 * BLOCK)
    sink = sinks.astype(jnp.float32).reshape(N_KV_HEADS, grp, 1, 1)
    scale = HEAD_DIM ** -0.5

    def one_block(args):
        qx, kx, vx, idx = args
        logits = jnp.einsum('bhgqd,bhkd->bhgqk', qx, kx, preferred_element_type=jnp.float32) * scale + bias
        valid = band & (idx * BLOCK - BLOCK + kj >= 0)
        logits = jnp.where(valid, logits, -jnp.inf)
        m = jnp.maximum(jnp.max(logits, axis=-1, keepdims=True), sink)
        p = jnp.exp(logits - m)
        p = p / (jnp.sum(p, axis=-1, keepdims=True) + jnp.exp(sink - m))
        return jnp.einsum('bhgqk,bhkd->bhgqd', p.astype(vx.dtype), vx)

    out = lax.map(one_block, (qb, kw, vw, jnp.arange(nb)))
    return out.transpose(1, 0, 4, 2, 3, 5).reshape(b, s, Q_W)

def memory_cross_attention(q, mem_k, mem_v):
    logits = jnp.einsum('bshd,bmhd->bhsm', q, mem_k, preferred_element_type=jnp.float32) * (X_HEAD_DIM ** -0.5)
    p = jax.nn.softmax(logits, axis=-1)
    out = jnp.einsum('bhsm,bmhd->bshd', p.astype(mem_v.dtype), mem_v)
    return out.reshape(q.shape[0], q.shape[1], XQ_W)

def causal_depthwise_conv(u, w, bias):
    out = lax.conv_general_dilated(u, w[:, None, :].astype(u.dtype), window_strides=(1,), padding=[(CONV_WIDTH - 1, 0)], dimension_numbers=('NWC', 'WIO', 'NWC'), feature_group_count=u.shape[-1])
    return out + bias.astype(u.dtype)

def ssd_chunked_scan(x, dt, a, bmat, cmat):
    b, s = x.shape[0], x.shape[1]
    nc = s // CHUNK

    def chunks(t):
        return t.reshape(b, nc, CHUNK, *t.shape[2:]).swapaxes(0, 1)

    causal = jnp.tril(jnp.ones((CHUNK, CHUNK), dtype=bool))

    def step(state, inp):
        xk, dtk, bk, ck = inp
        acum = jnp.cumsum(dtk * a, axis=1)
        at = acum.transpose(0, 2, 3, 1)
        decay = jnp.exp(jnp.where(causal, at[..., :, None] - at[..., None, :], -jnp.inf))
        cb = jnp.einsum('btgn,bsgn->bgts', ck, bk)
        xdt = xk * dtk[..., None]
        y_diag = jnp.einsum('bgets,bsgep->btgep', cb[:, :, None] * decay, xdt)
        y_off = jnp.einsum('btgn,bgepn->btgep', ck, state) * jnp.exp(acum)[..., None]
        to_end = jnp.exp(acum[:, -1:] - acum)
        new_state = state * jnp.exp(acum[:, -1])[..., None, None] + jnp.einsum('bsgn,bsge,bsgep->bgepn', bk, to_end, xdt)
        return new_state, y_diag + y_off

    state0 = jnp.zeros((b, N_SSM_GROUPS, HEADS_PER_GROUP, SSM_HEAD_DIM, D_STATE), jnp.float32)
    _, ys = lax.scan(step, state0, (chunks(x), chunks(dt), chunks(bmat), chunks(cmat)))
    return ys.swapaxes(0, 1).reshape(b, s, D_INNER)

def swa_mixer(h, mem_k, mem_v, w_in, sinks, w_out, rel_bias):
    b, s = h.shape[0], h.shape[1]
    q, k, v, xq = jnp.split(h @ w_in, [Q_W, Q_W + KV_W, Q_W + 2 * KV_W], axis=-1)
    attn = sliding_window_attention(q.reshape(b, s, N_Q_HEADS, HEAD_DIM), k.reshape(b, s, N_KV_HEADS, HEAD_DIM), v.reshape(b, s, N_KV_HEADS, HEAD_DIM), sinks, rel_bias)
    cross = memory_cross_attention(xq.reshape(b, s, N_X_HEADS, X_HEAD_DIM), mem_k, mem_v)
    return jnp.concatenate([attn, cross], axis=-1) @ w_out

def ssd_mixer(h, mem_k, mem_v, w_in, conv_w, conv_b, dt_bias, a_log, d_skip, g_norm, w_out):
    b, s = h.shape[0], h.shape[1]
    z, xbc, dt_raw, xq = jnp.split(h @ w_in, [D_INNER, D_INNER + CONV_CH, D_INNER + CONV_CH + N_SSM_HEADS], axis=-1)
    xbc = jax.nn.silu(causal_depthwise_conv(xbc, conv_w, conv_b))
    xs, bmat, cmat = jnp.split(xbc.astype(jnp.float32), [D_INNER, D_INNER + BC_W], axis=-1)
    dt = jax.nn.softplus(dt_raw.astype(jnp.float32) + dt_bias.astype(jnp.float32)).reshape(b, s, N_SSM_GROUPS, HEADS_PER_GROUP)
    a = -jnp.exp(a_log.astype(jnp.float32)).reshape(N_SSM_GROUPS, HEADS_PER_GROUP)
    xs = xs.reshape(b, s, N_SSM_GROUPS, HEADS_PER_GROUP, SSM_HEAD_DIM)
    y = ssd_chunked_scan(xs, dt, a, bmat.reshape(b, s, N_SSM_GROUPS, D_STATE), cmat.reshape(b, s, N_SSM_GROUPS, D_STATE))
    y = y + (xs * d_skip.astype(jnp.float32).reshape(N_SSM_GROUPS, HEADS_PER_GROUP, 1)).reshape(b, s, D_INNER)
    y = rmsnorm(y * jax.nn.silu(z.astype(jnp.float32)), g_norm).astype(h.dtype)
    cross = memory_cross_attention(xq.reshape(b, s, N_X_HEADS, X_HEAD_DIM), mem_k, mem_v)
    return jnp.concatenate([y, cross], axis=-1) @ w_out

def swiglu(h, wg, wu, wd):
    return (jax.nn.silu(h @ wg) * (h @ wu)) @ wd

def moe_swiglu(h, w_router, wg, wu, wd):
    b, s, d = h.shape
    logits = jnp.einsum('bsd,de->bse', h, w_router, preferred_element_type=jnp.float32)
    top_val, top_idx = lax.top_k(logits, TOP_K)
    gates = jax.nn.softmax(top_val, axis=-1)
    combine = jnp.sum(jax.nn.one_hot(top_idx, N_EXPERTS, dtype=jnp.float32) * gates[..., None], axis=-2)
    nb = s // BLOCK
    hb = h.reshape(b, nb, BLOCK, d).swapaxes(0, 1)
    cb = combine.reshape(b, nb, BLOCK, N_EXPERTS).swapaxes(0, 1)

    def one_block(args):
        hx, cx = args
        g = jnp.einsum('bqd,edf->bqef', hx, wg)
        u = jnp.einsum('bqd,edf->bqef', hx, wu)
        act = jax.nn.silu(g) * u * cx[..., None].astype(hx.dtype)
        return jnp.einsum('bqef,efd->bqd', act, wd)

    out = lax.map(one_block, (hb, cb))
    return out.swapaxes(0, 1).reshape(b, s, d)

def setup_inputs(seed: int = 0) -> dict:
    key = jax.random.key(seed)
    ks = iter(jax.random.split(key, 40))

    def nrm(shape, scale):
        return jax.random.normal(next(ks), shape, jnp.float32) * scale

    def gain(shape):
        return 1.0 + 0.02 * jax.random.normal(next(ks), shape, jnp.float32)

    inp = {}
    inp['x'] = nrm((BATCH, SEQ, D_MODEL), 1.0)
    inp['mem'] = nrm((BATCH, MEM_LEN, D_MODEL), 1.0)
    inp['g_mix'] = gain((DEPTH, D_MODEL))
    inp['g_ffn'] = gain((DEPTH, D_MODEL))
    inp['g_mem'] = gain((DEPTH, D_MODEL))
    inp['w_mem_kv'] = nrm((DEPTH, D_MODEL, 2 * XQ_W), D_MODEL ** -0.5)
    inp['rel_bias'] = nrm((N_BUCKETS, N_Q_HEADS), 0.5)
    inp['swa_w_in'] = nrm((N_EVEN, D_MODEL, SWA_IN_W), D_MODEL ** -0.5)
    inp['swa_sinks'] = nrm((N_EVEN, N_Q_HEADS), 1.0)
    inp['swa_w_out'] = nrm((N_EVEN, SWA_CAT_W, D_MODEL), SWA_CAT_W ** -0.5)
    inp['ssm_w_in'] = nrm((N_ODD, D_MODEL, SSM_IN_W), D_MODEL ** -0.5)
    inp['ssm_conv_w'] = nrm((N_ODD, CONV_WIDTH, CONV_CH), CONV_WIDTH ** -0.5)
    inp['ssm_conv_b'] = nrm((N_ODD, CONV_CH), 0.02)
    dt0 = jnp.exp(jax.random.uniform(next(ks), (N_ODD, N_SSM_HEADS), jnp.float32, minval=math.log(DT_MIN), maxval=math.log(DT_MAX)))
    inp['ssm_dt_bias'] = dt0 + jnp.log(-jnp.expm1(-dt0))
    inp['ssm_A_log'] = jnp.log(jax.random.uniform(next(ks), (N_ODD, N_SSM_HEADS), jnp.float32, minval=1.0, maxval=16.0))
    inp['ssm_D'] = 1.0 + 0.1 * jax.random.normal(next(ks), (N_ODD, N_SSM_HEADS), jnp.float32)
    inp['ssm_g_norm'] = gain((N_ODD, D_INNER))
    inp['ssm_w_out'] = nrm((N_ODD, SSM_CAT_W, D_MODEL), SSM_CAT_W ** -0.5)
    inp['ffn_w_gate'] = nrm((N_EVEN, D_MODEL, D_FF), D_MODEL ** -0.5)
    inp['ffn_w_up'] = nrm((N_EVEN, D_MODEL, D_FF), D_MODEL ** -0.5)
    inp['ffn_w_down'] = nrm((N_EVEN, D_FF, D_MODEL), D_FF ** -0.5)
    inp['moe_w_router'] = nrm((N_ODD, D_MODEL, N_EXPERTS), D_MODEL ** -0.5)
    inp['moe_w_gate'] = nrm((N_ODD, N_EXPERTS, D_MODEL, D_FF), D_MODEL ** -0.5)
    inp['moe_w_up'] = nrm((N_ODD, N_EXPERTS, D_MODEL, D_FF), D_MODEL ** -0.5)
    inp['moe_w_down'] = nrm((N_ODD, N_EXPERTS, D_FF, D_MODEL), D_FF ** -0.5)
    inp['g_final'] = gain((D_MODEL,))
    return inp

def reference(x, mem, g_mix, g_ffn, g_mem, w_mem_kv, rel_bias, swa_w_in, swa_sinks, swa_w_out, ssm_w_in, ssm_conv_w, ssm_conv_b, ssm_dt_bias, ssm_A_log, ssm_D, ssm_g_norm, ssm_w_out, ffn_w_gate, ffn_w_up, ffn_w_down, moe_w_router, moe_w_gate, moe_w_up, moe_w_down, g_final):
    b, m = mem.shape[0], mem.shape[1]
    for i in range(DEPTH):
        j = i // 2
        mem_kv = rmsnorm(mem, g_mem[i]) @ w_mem_kv[i]
        mem_k = mem_kv[..., :XQ_W].reshape(b, m, N_X_HEADS, X_HEAD_DIM)
        mem_v = mem_kv[..., XQ_W:].reshape(b, m, N_X_HEADS, X_HEAD_DIM)
        h = rmsnorm(x, g_mix[i])
        if i % 2 == 0:
            x = x + swa_mixer(h, mem_k, mem_v, swa_w_in[j], swa_sinks[j], swa_w_out[j], rel_bias)
            x = x + swiglu(rmsnorm(x, g_ffn[i]), ffn_w_gate[j], ffn_w_up[j], ffn_w_down[j])
        else:
            x = x + ssd_mixer(h, mem_k, mem_v, ssm_w_in[j], ssm_conv_w[j], ssm_conv_b[j], ssm_dt_bias[j], ssm_A_log[j], ssm_D[j], ssm_g_norm[j], ssm_w_out[j])
            x = x + moe_swiglu(rmsnorm(x, g_ffn[i]), moe_w_router[j], moe_w_gate[j], moe_w_up[j], moe_w_down[j])
    return rmsnorm(x, g_final)


_drawn_inputs = setup_inputs


def setup_inputs(seed=0):
    import zlib

    import numpy as np

    out = dict(_drawn_inputs(seed))
    spreads = {}
    factors = {'g_mem': 8.0,
     'swa_sinks': 11.427,
     'ssm_g_norm': 22.327,
     'g_final': 7.863,
     'g_ffn': 5.499,
     'ssm_conv_b': 5.429,
     'ssm_D': 3.242}
    for name, (base, spread) in spreads.items():
        noise = np.random.default_rng([zlib.crc32(name.encode()), seed]).standard_normal(out[name].shape)
        drawn = base * np.exp(spread * noise) if base else spread * noise
        out[name] = jnp.asarray(drawn.astype(out[name].dtype))
    for name, factor in factors.items():
        out[name] = (out[name] * factor).astype(out[name].dtype)
    return out
```

```python
import math
from contextlib import ExitStack

import numpy as np

import concourse.bass as bass
from concourse import mybir

F32 = mybir.dt.float32
ALU = mybir.AluOpType
ACT = mybir.ActivationFunctionType
AX_X = mybir.AxisListType.X

P = 128
D = 1024
KD = D // P
NT = 2
S = NT * P
EPS = 1e-6
NEG = -1e30

HQ, HD = 16, 64
NB, MAX_DIST = 32, 128
HX, XD = 4, 256
DI = 2048
KI = DI // P
NH = 32
G, HPG, PH = 4, 8, 64
KBC = 8
CW = 4
FF = 2816
NE = 8
FC = FF // 256

PC_MIX, PC_FFN, PC_MEM = 0, 16, 32
PC_CW = 48
PC_CB = PC_CW + 24 * CW
PC_GN = PC_CB + 24
PC_RT = PC_GN + KI
PC_N = PC_RT + KD * NE
PR_SINK, PR_DTB, PR_ALOG, PR_D, PR_GF = 0, 16, 48, 80, 112
PR_N = PR_GF + D
C_ID, C_TRI, C_SU, C_J, C_ONE, C_LT, C_N = 0, 128, 256, 384, 512, 640, 704

RING = 3
UNIT = 2048


def constants():
    c = np.zeros((P, C_N), np.float32)
    i, j = np.arange(P)[:, None], np.arange(P)[None, :]
    c[:, C_ID:C_ID + P] = i == j
    c[:, C_TRI:C_TRI + P] = i <= j
    c[:, C_SU:C_SU + P] = i > j
    c[:, C_J:C_J + P] = i + j == P - 1
    c[:, C_ONE:C_ONE + P] = 1.0
    e = np.arange(NE)
    c[:, C_LT:C_LT + 64] = (e[None, :] < e[:, None]).astype(np.float32).reshape(1, 64)
    return c


def bucket_rows():
    d = np.arange(P - 1, -1, -1)
    half = NB // 2
    far = half + (np.log(np.maximum(d, 1).astype(np.float32) / np.float32(half)) / np.float32(math.log(MAX_DIST / half))
                  * np.float32(NB - half)).astype(np.int32)
    b = np.where(d < half, d, np.minimum(far, NB - 1))
    return (np.arange(NB)[:, None] == b[None, :]).astype(np.float32)


def weight_units(a):
    def cols(w, c0, n):
        return w.rearrange("(t p) n -> p t n", p=P)[:, :, c0:c0 + n]

    def kb(w, kg, n):
        return w.rearrange("(t p) n -> p t n", p=P)[:, 4 * kg:4 * kg + 4, 512 * n:512 * n + 512]

    u0, u1 = [], []
    for layer, u in ((0, u0), (1, u1)):
        mk = a["w_mem_kv"][layer]
        u += [(cols(mk, 256 * j, 256), "a") for j in range(4)]
        u += [(kb(mk, kg, 2 + n), "b") for n in range(2) for kg in range(2)]
    w = a["swa_w_in"][0]
    u0 += [(cols(w, 256 * j, 256), "a") for j in range(9)]
    u0 += [(kb(a["swa_w_out"][0], kg, n), "b") for n in range(2) for kg in range(4)]
    w = a["ssm_w_in"][0]
    u1 += [(cols(w, DI + 3072 + NH + 256 * j, 256), "a") for j in range(4)]
    u1 += [(cols(w, DI + 3072, NH), "t")]
    u1 += [(cols(w, 2 * DI + 256 * j, 256), "a") for j in range(4)]
    u1 += [(cols(w, DI + 256 * j, 256), "a") for j in range(8)]
    u1 += [(kb(w, kg, n), "b") for n in range(4) for kg in range(2)]
    u1 += [(kb(a["ssm_w_out"][0], kg, n), "b") for n in range(2) for kg in range(6)]
    return u0, u1


def trunk(nc, a, out):
    u0, u1 = weight_units(a)
    FFN0 = len(u0)
    L1 = FFN0 + 3 * FC
    MOE = L1 + len(u1)
    static = {n: x for n, x in enumerate(u0)} | {L1 + n: x for n, x in enumerate(u1)}

    ctx = ExitStack()
    with ctx:
        def sb(name, shape):
            return ctx.enter_context(nc.sbuf_tensor(name, shape, F32))

        def sem(name):
            return ctx.enter_context(nc.semaphore(name))

        ring = sb("ring", [P, RING, UNIT])
        x = sb("x", [P, NT, D])
        mem = sb("mem", [P, NT, D])
        xn = sb("xn", [P, NT, D])
        hT = sb("hT", [P, KD, S])
        memT = sb("memT", [P, KD, S])
        memK = sb("memK", [P, KD, S])
        memV = sb("memV", [P, NT, D])
        xqT = sb("xqT", [P, KD, S])
        cat = sb("cat", [P, 24, S])
        prob = sb("prob", [P, 2, 2, S])
        probT = sb("probT", [P, 2, 2 * S])
        act = sb("act", [P, 2, 2, S])
        con = sb("con", [P, C_N])
        pc = sb("pc", [P, PC_N])
        pr = sb("pr", [P, PR_N])
        stat = sb("stat", [P, 64])
        ssq, var, rstd = sb("ssq", [P, 16]), sb("var", [P, 16]), sb("rstd", [P, 16])
        mhalf = sb("mhalf", [P, 1])
        nsink = sb("nsink", [P, HQ])
        mx, nm, sd, es, sm, den, rden = (sb(n, [P, 2, 2]) for n in ("mx", "nm", "sd", "es", "sm", "den", "rden"))
        rel = sb("rel", [NB, HQ])
        buck = sb("buck", [NB, P])
        brow = sb("brow", [HQ, 384])
        lg = sb("lg", [P, NT, NE])
        cmp1, cmp2 = sb("cmp1", [P, NT, NE, NE]), sb("cmp2", [P, NT, NE, NE])
        rank, top, nv1, pe8, comb = (sb(n, [P, NT, NE]) for n in ("rank", "top", "nv1", "pe8", "comb"))
        s8 = sb("s8", [P, NT])

        with ExitStack() as l0:
            def sb0(name, shape):
                return l0.enter_context(nc.sbuf_tensor(name, shape, F32))
            hankel = sb0("hankel", [P, HQ, S])
            qT = sb0("qT", [P, KD, S])
            kz = sb0("kz", [P, 2, 2, S])
            vz = sb0("vz", [P, NT, 2, 192])
        BCT = sb("BCT", [P, KBC, S])
        y = sb("y", [P, NT, DI])
        ub = sb("ub", [P, 2, 2, S + CW - 1])
        cv = sb("cv", [P, 2, S])
        xcT = sb("xcT", [P, 2, 2, S])
        dtx, dtu, dtr_, dtm, dt, dta = (sb(n, [P, NT, NH]) for n in ("dtx", "dtu", "dtr", "dtm", "dt", "dta"))
        na = sb("na", [P, NH])
        eac, toe = sb("eac", [P, NH]), sb("toe", [P, NH])
        Lm = sb("Lm", [P, 2, 4, P])
        dec = sb("dec", [P, 2, 4, P])
        cbm = sb("cbm", [P, P])
        btok = sb("btok", [P, P])
        xdt = sb("xdt", [P, HPG, PH])
        xde = sb("xde", [P, HPG, PH])
        xsD = sb("xsD", [P, HPG, PH])
        yo = sb("yo", [P, 512])
        st = sb("st", [P, G, 512])
        zs = sb("zs", [P, 2, 512])

        PB = [ctx.enter_context(nc.psum_tensor(f"PB{i}", [P, 512], F32)) for i in range(8)]
        brow_dram = nc.dram_tensor("brow_dram", (HQ, 384), F32, kind="Internal").ap()

        names = """x_in mem_in par_in rel_in brow_set brow_st hank_in stores
            units_used mhalf_set nsink_set bias_full brow_done kz_zero vz_zero
            sq_done var_done rstd_done xn_done tr_full tr_drained
            s_full mx_done nm_done sd_done exp_done es_done den_done rden_done p_ready t_full pT_ready o_full cat_done
            qk_ready
            silu_done act_done y_drained
            dt_chain dt_ready ln_chain dta_full eac_done u_zero u_ready conv_chain conv_done silu_conv xT_full xs_ready
            cb_full cbm_done l_ready seg_full dec_done m_ready bt_full btok_done st_full st_done
            xdt_ready xde_ready xsD_ready yd_full yo_full yo_done yy_done yg_done zs_done ynorm
            rt_full lg_done rt_chain rt_exp comb_ready final fin_sq""".split()
        q = {n: sem(n) for n in names}
        raw_in = [sem(f"raw_in{i}") for i in range(RING)]
        drained = [sem(f"drained{i}") for i in range(4)]

        ident = con[:, C_ID:C_ID + P]
        tri = con[:, C_TRI:C_TRI + P]
        su = con[:, C_SU:C_SU + P]
        antiJ = con[:, C_J:C_J + P]
        block = ctx.enter_context(nc.Block())

        def unit_view(n, kind):
            r = ring[:, n % RING, :]
            if kind == "a":
                return r.rearrange("p (k c) -> p k c", k=8)
            if kind == "b":
                return r.rearrange("p (k c) -> p k c", k=4)
            if kind == "d":
                return r.rearrange("p (k c) -> p k c", k=2)
            return r[:, 0:8 * NH].rearrange("p (k c) -> p k c", k=8)

        def unit_landed(eng, n, turn=0):
            eng.wait_ge(raw_in[n % RING], 16 * (n // RING + 1) + turn * (16 * 3 * FC // RING))

        R_MEM0, R_H0, R_F0, R_MEM1, R_H1, R_Y, R_F1, R_FIN = range(8)
        TR_BEFORE = {R_MEM0: 0, R_H0: 4, R_F0: 8, R_MEM1: 12, R_H1: 16, R_Y: 20, R_F1: 28}

        fills, last_unit = {}, []
        for name, start, n, per in (("k0", 0, 4, 1), ("v0", 4, 4, 2), ("q", 8, 4, 1), ("kv", 12, 1, 1), ("xq0", 13, 4, 1), ("out0", 17, 4, 4),
                                    ("k1", L1, 4, 1), ("v1", L1 + 4, 4, 2), ("xq1", L1 + 8, 4, 1), ("dt", L1 + 12, 1, 1),
                                    ("bc", L1 + 13, 4, 1), ("x", L1 + 17, 8, 1), ("z", L1 + 25, 8, 2), ("out1", L1 + 33, 4, 6)):
            fills[name] = len(last_unit)
            last_unit += [start + j if per == 1 else start + per * (j // NT) + per - 1 for j in range(n)]
        FFN_TURNS = 1 + NE

        def fill_ready(eng, f):
            eng.wait_ge(q["units_used"], last_unit[f] + 1)

        def fills_drained(eng, name):
            end = fills[name] + {"out0": 4, "out1": 4, "xq0": 4, "xq1": 4, "x": 8}[name]
            for f in range(end - 4, end):
                eng.wait_ge(drained[f % 4], f // 4 + 1)

        def ffn_at(c, part):
            if part == 2:
                return 3 * c + 4 if c < FC - 1 else 3 * FC - 1
            return max(3 * c - 1, 0) + part

        def ffn_turn(turn):
            return (FFN0, 0) if isinstance(turn, int) else (MOE, turn - 1)

        @block.sync
        def _(sp):
            sp.dma_start(mem[:, :, :], a["mem"][0].rearrange("(t p) d -> p t d", p=P)).then_inc(q["mem_in"], 16)
            sp.dma_start(pc[:, :], a["pcol"]).then_inc(q["par_in"], 16)
            sp.dma_start(con[:, :], a["const"]).then_inc(q["par_in"], 16)
            sp.dma_start(pr[:, :], a["prow"].partition_broadcast(P).rearrange("p a n -> p (a n)")).then_inc(q["par_in"], 16)
            sp.dma_start(x[:, :, :], a["x"][0].rearrange("(t p) d -> p t d", p=P)).then_inc(q["x_in"], 16)

            def load(n, src, kind):
                if n >= RING:
                    sp.wait_ge(q["units_used"], n - RING + 1)
                sp.dma_start(unit_view(n, kind), src).then_inc(raw_in[n % RING], 16)

            for n in range(RING):
                load(n, *static[n])
            sp.dma_start(rel[:, :], a["rel_bias"]).then_inc(q["rel_in"], 16)
            sp.dma_start(buck[:, :], a["bucket"]).then_inc(q["rel_in"], 16)
            sp.wait_ge(q["brow_done"], 1)
            sp.dma_start(brow_dram, brow[:, :]).then_inc(q["brow_st"], 16)
            sp.wait_ge(q["brow_st"], 16)
            sp.dma_start(hankel[:, :, :], bass.AP(brow_dram.tensor, 0, [[1, P], [384, HQ], [1, S]])).then_inc(q["hank_in"], 16)
            for n in range(RING, FFN0):
                load(n, *static[n])

            def ffn_loads(u, turn, wg, wu, wd):
                units = sorted((ffn_at(c, part), c, part) for c in range(FC) for part in range(3))
                for at, c, part in units:
                    src = (wg[:, :, 256 * c:256 * c + 256], wu[:, :, 256 * c:256 * c + 256], wd[:, 2 * c:2 * c + 2, :])[part]
                    sp.wait_ge(q["units_used"], u + at - RING + 1 + turn * (3 * FC))
                    sp.dma_start(unit_view(u + at, "aad"[part]), src).then_inc(raw_in[(u + at) % RING], 16)

            def kpn(w):
                return w.rearrange("(t p) n -> p t n", p=P)

            ffn_loads(FFN0, 0, kpn(a["ffn_w_gate"][0]), kpn(a["ffn_w_up"][0]), kpn(a["ffn_w_down"][0]))
            for n in range(L1, MOE):
                load(n, *static[n])
            with sp.Fori(0, NE) as e:
                def expert(w):
                    return w[0, bass.ds(e, 1)].rearrange("e (t p) n -> p (e t) n", p=P)
                ffn_loads(MOE, e, expert(a["moe_w_gate"]), expert(a["moe_w_up"]), expert(a["moe_w_down"]))
            sp.wait_ge(q["final"], 2)
            sp.dma_start(out[0].rearrange("(t p) d -> p t d", p=P), xn[:, :, :]).then_inc(q["stores"], 16)
            sp.wait_ge(q["stores"], 16)

        @block.gpsimd
        def _(pool):
            pool.memset(mhalf[:, :], -0.5).then_inc(q["mhalf_set"], 1)
            pool.memset(kz[:, :, :, :], 0.0).then_inc(q["kz_zero"], 1)
            pool.memset(vz[:, :, :, :], 0.0).then_inc(q["kz_zero"], 1)
            pool.wait_ge(q["mhalf_set"], 1)

            def rms(r, width):
                for t in range(NT):
                    c = 2 * r + t
                    pool.wait_ge(q["sq_done"], c + 1)
                    pool.tensor_scalar(var[:, c:c + 1], ssq[:, c:c + 1], 1.0 / width, EPS, ALU.mult, ALU.add).then_inc(q["var_done"], 1)
                    pool.wait_ge(q["var_done"], c + 1)
                    pool.tensor_tensor(rstd[:, c:c + 1], var[:, c:c + 1], mhalf[:, :], ALU.pow).then_inc(q["rstd_done"], 1)

            for r in (R_MEM0, R_H0, R_F0, R_MEM1, R_H1):
                rms(r, D)

            pool.wait_ge(q["dt_ready"], 1)
            pool.wait_ge(q["par_in"], 48)
            for s in range(2 * G):
                c, g = divmod(s, G)
                xs = y[:, c, 512 * g:512 * g + 512].rearrange("p (h d) -> p h d", h=HPG)
                for half in range(2):
                    h0 = HPG * g + 4 * half
                    n = 2 * s + half
                    if n >= 2:
                        pool.wait_ge(q["seg_full"], n - 1)
                    pool.tensor_tensor(Lm[:, n % 2], su.unsqueeze(1).to_broadcast([P, 4, P]),
                                       dta[:, c, h0:h0 + 4].unsqueeze(2).to_broadcast([P, 4, P]), ALU.mult).then_inc(q["l_ready"], 1)
                if s == 0:
                    pool.wait_ge(q["xs_ready"], 8)
                    pool.wait_ge(q["eac_done"], 2)
                if s >= 1:
                    pool.wait_ge(q["yd_full"], s)
                pool.tensor_tensor(xdt[:, :, :], xs, dt[:, c, HPG * g:HPG * g + HPG].unsqueeze(2).to_broadcast([P, HPG, PH]),
                                   ALU.mult).then_inc(q["xdt_ready"], 1)
                if c == 0:
                    pool.wait_ge(q["xdt_ready"], s + 1)
                    if s >= 1:
                        pool.wait_ge(q["st_full"], s)
                    pool.tensor_tensor(xde[:, :, :], xdt[:, :, :], toe[:, HPG * g:HPG * g + HPG].unsqueeze(2).to_broadcast([P, HPG, PH]),
                                       ALU.mult).then_inc(q["xde_ready"], 1)
                if s >= 1:
                    pool.wait_ge(q["yy_done"], s)
                pool.tensor_tensor(xsD[:, :, :], xs, pr[:, PR_D + HPG * g:PR_D + HPG * g + HPG].unsqueeze(2).to_broadcast([P, HPG, PH]),
                                   ALU.mult).then_inc(q["xsD_ready"], 1)
            rms(R_Y, DI)
            rms(R_F1, D)
            rms(R_FIN, D)

        @block.scalar
        def _(ac):
            def square_sum(r, src, dump):
                for t in range(NT):
                    if t or r:
                        ac.wait_ge(q["sq_done"], 2 * r + t)
                    nc.scalar.activation(dump, src[:, t, :], ACT.Square,
                                         accum_out=ssq[:, 2 * r + t:2 * r + t + 1]).then_inc(q["sq_done"], 1)

            def gemm_out(f, dst, scale=1.0, func=ACT.Copy, cols=slice(0, 512), parts=slice(0, P), free=True):
                fill_ready(ac, f)
                i = nc.scalar.activation(dst, PB[f % 4][parts, cols], func, scale=scale)
                if free:
                    i.then_inc(drained[f % 4], 1)
                return i

            def exp_step(s, swa):
                w = P if swa and s < 8 else S
                ac.wait_ge(q["nm_done"], s + 1)
                if s >= 2:
                    ac.wait_ge(q["t_full"], s - 1)
                    ac.wait_ge(q["p_ready"], s - 1)
                bank = PB[4 + s % 2][:, :].rearrange("p (j k) -> p j k", j=2)
                for j in range(2):
                    nc.scalar.activation(prob[:, s % 2, j, 0:w], bank[:, j, 0:w], ACT.Exp, bias=nm[:, s % 2, j:j + 1],
                                         accum_out=sm[:, s % 2, j:j + 1]).then_inc(q["exp_done"], 1)
                if swa:
                    ac.wait_ge(q["sd_done"], s + 1)
                    nc.scalar.activation(es[:, s % 2, :], sd[:, s % 2, :], ACT.Exp).then_inc(q["es_done"], 1)

            def probT_step(s, swa):
                w = 256 if swa and s < 8 else 512
                ac.wait_ge(q["t_full"], s + 1)
                if s >= 2:
                    ac.wait_ge(q["o_full"], s - 1)
                nc.scalar.activation(probT[:, s % 2, 0:w], PB[6][:, 0:w], ACT.Copy).then_inc(q["pT_ready"], 1)

            def softmax_steps(first, last, swa):
                exp_step(first, swa(first))
                for s in range(first, last):
                    if s + 1 < last:
                        exp_step(s + 1, swa(s + 1))
                    probT_step(s, swa(s))

            def memory_kv(layer):
                for j in range(4):
                    gemm_out(fills[f"k{layer}"] + j, memK[:, 2 * j:2 * j + 2, :])
                for n in range(2):
                    for t in range(NT):
                        gemm_out(fills[f"v{layer}"] + 2 * n + t, memV[:, t, 512 * n:512 * n + 512])

            def cross_q(layer):
                for j in range(4):
                    i = gemm_out(fills[f"xq{layer}"] + j, xqT[:, 2 * j:2 * j + 2, :], scale=XD ** -0.5, free=False)
                    i.then_inc(drained[(fills[f"xq{layer}"] + j) % 4], 1)

            def ffn_silu(turn):
                u, t33 = ffn_turn(turn)
                for c in range(FC):
                    ac.wait_ge(q["units_used"], u + ffn_at(c, 0) + 1 + t33 * (3 * FC))
                    nc.scalar.activation(act[:, c % 2].rearrange("p k s -> p (k s)"), PB[2 * (c % 2)][:, :], ACT.Silu).then_inc(q["silu_done"], 1)

            ac.wait_ge(q["mem_in"], 16)
            square_sum(R_MEM0, mem, cat[:, 0:4, :].rearrange("p a b -> p (a b)"))
            ac.wait_ge(q["x_in"], 16)
            square_sum(R_H0, x, cat[:, 0:4, :].rearrange("p a b -> p (a b)"))
            memory_kv(0)
            for j in range(4):
                gemm_out(fills["q"] + j, qT[:, 2 * j:2 * j + 2, :], scale=HD ** -0.5)
            f = fills["kv"]
            fill_ready(ac, f)
            ac.wait_ge(q["kz_zero"], 2)
            for kv in range(2):
                for half in range(2):
                    nc.scalar.activation(kz[64 * half:64 * half + 64, kv, half, :], PB[f % 4][64 * kv:64 * kv + 64, 0:S],
                                         ACT.Copy).then_inc(q["qk_ready"], 1)
            for t in range(NT):
                i = nc.scalar.activation(vz[:, t, :, 64:128], PB[f % 4][:, 256 + 128 * t:384 + 128 * t].rearrange("p (v d) -> p v d", v=2), ACT.Copy)
                i.then_inc(drained[f % 4] if t == 1 else q["qk_ready"], 1)
            softmax_steps(0, 16, lambda s: True)
            cross_q(0)
            softmax_steps(16, 20, lambda s: False)
            fills_drained(ac, "out0")
            square_sum(R_F0, x, cat[:, 16:20, :].rearrange("p a b -> p (a b)"))
            ffn_silu(0)

            square_sum(R_MEM1, mem, cat[:, 16:20, :].rearrange("p a b -> p (a b)"))
            ac.wait_ge(q["y_drained"], 1)
            square_sum(R_H1, x, cat[:, 16:20, :].rearrange("p a b -> p (a b)"))
            memory_kv(1)
            cross_q(1)
            softmax_steps(20, 24, lambda s: False)

            nc.scalar.activation(na[:, :], pr[:, PR_ALOG:PR_ALOG + NH], ACT.Exp).then_inc(q["ln_chain"], 1)
            ac.wait_ge(q["dt_chain"], 2)
            nc.scalar.activation(dtu[:, :, :], dtr_[:, :, :], ACT.Exp, scale=-1.0).then_inc(q["ln_chain"], 1)
            ac.wait_ge(q["dt_chain"], 3)
            nc.scalar.activation(dtr_[:, :, :], dtm[:, :, :], ACT.Ln).then_inc(q["ln_chain"], 1)
            ac.wait_ge(q["dta_full"], 1)
            nc.scalar.activation(eac[:, :], PB[4][:, 0:NH], ACT.Exp).then_inc(q["eac_done"], 1)
            nc.scalar.activation(toe[:, :], PB[4][:, 64:64 + NH], ACT.Exp).then_inc(q["eac_done"], 1)
            ac.wait_ge(q["u_zero"], 1)
            for j in range(12):
                f = fills["bc"] + j if j < 4 else fills["x"] + j - 4
                if j >= 2:
                    ac.wait_ge(q["conv_done"], 2 * (j - 1))
                fill_ready(ac, f)
                nc.scalar.activation(ub[:, j % 2, :, CW - 1:], PB[f % 4][:, :].rearrange("p (a b) -> p a b", a=2), ACT.Copy).then_inc(drained[f % 4], 1)
                for k in range(2):
                    ac.wait_ge(q["conv_done"], 2 * j + k + 1)
                    if j < 4:
                        dst = BCT[:, 2 * j + k, :]
                    else:
                        if j >= 6:
                            ac.wait_ge(q["xT_full"], j - 5)
                        dst = xcT[:, j % 2, k, :]
                    nc.scalar.activation(dst, cv[:, k, :], ACT.Silu).then_inc(q["silu_conv"], 1)
                if j >= 4:
                    ac.wait_ge(q["xT_full"], j - 3)
                    nc.scalar.activation(y[:, :, 256 * (j - 4):256 * (j - 3)], PB[6][:, :].rearrange("p (t c) -> p t c", t=NT),
                                         ACT.Copy).then_inc(q["xs_ready"], 1)
            for s in range(2 * G):
                c, g = divmod(s, G)
                for half in range(2):
                    n = 2 * s + half
                    ac.wait_ge(q["seg_full"], n + 1)
                    if n >= 2:
                        ac.wait_ge(q["yd_full"], n // 2)
                    nc.scalar.activation(dec[:, n % 2].rearrange("p h t -> p (h t)"), PB[4 + n % 2][:, :], ACT.Exp).then_inc(q["dec_done"], 1)
                    if c == 0 and half == 0:
                        ac.wait_ge(q["bt_full"], s + 1)
                        nc.scalar.activation(btok[:, :], PB[7][:, 256:384], ACT.Copy).then_inc(q["btok_done"], 1)
                if c == 0:
                    ac.wait_ge(q["st_full"], s + 1)
                    nc.scalar.activation(st[:, g, :], PB[6][:, :], ACT.Copy).then_inc(q["st_done"], 1)
            for n in range(4):
                for t in range(NT):
                    i = 2 * n + t
                    if i >= 2:
                        ac.wait_ge(q["yg_done"], i - 1)
                    gemm_out(fills["z"] + i, zs[:, i % 2, :], func=ACT.Silu, free=False).then_inc(drained[(fills["z"] + i) % 4], 1)
                    ac.wait_ge(drained[(fills["z"] + i) % 4], (fills["z"] + i) // 4 + 1)
            ac.wait_ge(q["yg_done"], 8)
            for t in range(NT):
                ac.wait_ge(q["sq_done"], 2 * R_Y + t)
                nc.scalar.activation(st[:, :, :].rearrange("p a b -> p (a b)"), y[:, t, :], ACT.Square,
                                     accum_out=ssq[:, 2 * R_Y + t:2 * R_Y + t + 1]).then_inc(q["sq_done"], 1)
            fills_drained(ac, "out1")
            square_sum(R_F1, x, cat[:, 20:24, :].rearrange("p a b -> p (a b)"))
            ac.wait_ge(q["rt_chain"], 6)
            nc.scalar.activation(pe8[:, :, :], nv1[:, :, :], ACT.Exp).then_inc(q["rt_exp"], 1)
            with ac.Fori(1, FFN_TURNS) as turn:
                ffn_silu(turn)
            ac.wait_ge(q["y_drained"], FFN_TURNS)
            square_sum(R_FIN, x, cat[:, 20:24, :].rearrange("p a b -> p (a b)"))

        @block.vector
        def _(ve):
            def norm_T(r, src, g0, dst, width, into):
                nk = width // P
                for t in range(NT):
                    c = 2 * r + t
                    ve.wait_ge(q["rstd_done"], c + 1)
                    ve.tensor_scalar(into[:, t, :], src[:, t, :], rstd[:, c:c + 1], None, ALU.mult).then_inc(q["xn_done"], 1)
                f = TR_BEFORE[r]
                for t in range(NT):
                    for k in range(0, nk, 4):
                        ve.wait_ge(q["tr_full"], f + 1)
                        ve.tensor_tensor(dst[:, k:k + 4, P * t:P * t + P], PB[4 + f % 2][:, :].rearrange("p (k s) -> p k s", k=4),
                                         pc[:, g0 + k:g0 + k + 4].unsqueeze(2).to_broadcast([P, 4, P]), ALU.mult).then_inc(q["tr_drained"], 1)
                        f += 1

            def max_step(s, swa):
                w = P if swa and s < 8 else S
                ve.wait_ge(q["s_full"], s + 1)
                bank = PB[4 + s % 2][:, :].rearrange("p (j k) -> p j k", j=2)[:, :, 0:w]
                if s >= 2:
                    ve.wait_ge(q["exp_done"], 2 * (s - 1))
                if swa:
                    ve.tensor_reduce(mx[:, s % 2, :], bank, AX_X, ALU.max).then_inc(q["mx_done"], 1)
                    ve.wait_ge(q["mx_done"], s + 1)
                    ve.scalar_tensor_tensor(out=nm[:, s % 2, :], in0=mx[:, s % 2, :], scalar=-1.0,
                                            in1=nsink[:, 2 * (s % 8):2 * (s % 8) + 2], op0=ALU.mult, op1=ALU.min).then_inc(q["nm_done"], 1)
                    ve.wait_ge(q["nm_done"], s + 1)
                    if s >= 2:
                        ve.wait_ge(q["es_done"], s - 1)
                    ve.tensor_tensor(sd[:, s % 2, :], nm[:, s % 2, :], nsink[:, 2 * (s % 8):2 * (s % 8) + 2], ALU.subtract).then_inc(q["sd_done"], 1)
                else:
                    ve.tensor_reduce(nm[:, s % 2, :], bank, AX_X, ALU.max, negate=True).then_inc(q["nm_done"], 1)

            def norm_step(s, swa):
                w = P if swa and s < 8 else S
                ve.wait_ge(q["exp_done"], 2 * s + 2)
                if swa:
                    ve.wait_ge(q["es_done"], s + 1)
                    ve.tensor_tensor(den[:, s % 2, :], sm[:, s % 2, :], es[:, s % 2, :], ALU.add).then_inc(q["den_done"], 1)
                    ve.wait_ge(q["den_done"], s + 1)
                    ve.reciprocal(rden[:, s % 2, :], den[:, s % 2, :]).then_inc(q["rden_done"], 1)
                else:
                    ve.reciprocal(rden[:, s % 2, :], sm[:, s % 2, :]).then_inc(q["rden_done"], 1)
                ve.wait_ge(q["rden_done"], s + 1)
                pv = prob[:, s % 2, :, 0:w]
                ve.tensor_tensor(pv, pv, rden[:, s % 2, :].unsqueeze(2).to_broadcast([P, 2, w]), ALU.mult).then_inc(q["p_ready"], 1)

            def cat_step(s, tile0):
                ve.wait_ge(q["o_full"], s + 1)
                if s < 16:
                    i = ve.tensor_copy(cat[:, s % 8, P * (s // 8):P * (s // 8) + P], PB[7][:, 0:P])
                else:
                    i = ve.tensor_copy(cat[:, tile0:tile0 + 2, :], PB[7][:, :].rearrange("p (a b) -> p a b", a=2))
                i.then_inc(q["cat_done"], 1)

            def softmax_steps(first, last, swa, tile0=0):
                max_step(first, swa)
                for s in range(first, last):
                    if s + 1 < last:
                        max_step(s + 1, swa)
                    norm_step(s, swa)
                    if s > first:
                        cat_step(s - 1, tile0 + 2 * (s - 1 - first))
                cat_step(last - 1, tile0 + 2 * (last - 1 - first))

            def add_out(name):
                for n in range(2):
                    for t in range(NT):
                        f = fills[name] + 2 * n + t
                        fill_ready(ve, f)
                        xv = x[:, t, 512 * n:512 * n + 512]
                        ve.tensor_tensor(xv, xv, PB[f % 4][:, :], ALU.add).then_inc(drained[f % 4], 1)
                fills_drained(ve, name)

            def ffn_mul(turn):
                u, t33 = ffn_turn(turn)
                for c in range(FC):
                    ve.wait_ge(q["units_used"], u + ffn_at(c, 1) + 1 + t33 * (3 * FC))
                    ve.wait_ge(q["silu_done"], c + 1 + turn * FC)
                    av = act[:, c % 2].rearrange("p k s -> p (k s)")
                    ve.tensor_tensor(av, av, PB[2 * (c % 2) + 1][:, :], ALU.mult).then_inc(q["act_done"], 1)
                ve.wait_ge(q["units_used"], u + 3 * FC + t33 * (3 * FC))
                for t in range(NT):
                    for n in range(2):
                        xv = x[:, t, 512 * n:512 * n + 512]
                        bank = PB[4 + 2 * n + t][:, :]
                        if isinstance(turn, int):
                            i = ve.tensor_tensor(xv, xv, bank, ALU.add)
                        else:
                            i = ve.scalar_tensor_tensor(out=xv, in0=bank, scalar=comb[:, t, bass.ds(turn - 1, 1)], in1=xv, op0=ALU.mult, op1=ALU.add)
                i.then_inc(q["y_drained"], 1)

            ve.wait_ge(q["par_in"], 48)
            ve.tensor_scalar(nsink[:, :], pr[:, PR_SINK:PR_SINK + HQ], -1.0, None, ALU.mult).then_inc(q["nsink_set"], 1)
            ve.memset(brow[:, :], NEG).then_inc(q["brow_set"], 1)
            ve.wait_ge(q["mem_in"], 16)
            norm_T(R_MEM0, mem, PC_MEM, memT, D, xn)
            ve.wait_ge(q["bias_full"], 1)
            ve.wait_ge(q["brow_set"], 1)
            ve.tensor_copy(brow[:, P:2 * P], PB[6][0:HQ, 0:P]).then_inc(q["brow_done"], 1)
            ve.wait_ge(q["x_in"], 16)
            ve.wait_ge(q["tr_full"], 4)
            norm_T(R_H0, x, PC_MIX, hT, D, xn)
            ve.wait_ge(q["nsink_set"], 1)
            softmax_steps(0, 16, True)
            softmax_steps(16, 20, False, 8)
            add_out("out0")
            norm_T(R_F0, x, PC_FFN, hT, D, xn)
            ffn_mul(0)
            norm_T(R_MEM1, mem, PC_MEM + 8, memT, D, xn)
            ve.wait_ge(q["y_drained"], 1)
            ve.wait_ge(q["tr_full"], 16)
            norm_T(R_H1, x, PC_MIX + 8, hT, D, xn)
            softmax_steps(20, 24, False, 16)

            f = fills["dt"]
            fill_ready(ve, f)
            ve.tensor_tensor(dtx[:, :, :], PB[f % 4][:, 0:64].rearrange("p (t h) -> p t h", t=NT),
                             pr[:, PR_DTB:PR_DTB + NH].unsqueeze(1).to_broadcast([P, NT, NH]), ALU.add).then_inc(drained[f % 4], 1)
            ve.wait_ge(drained[f % 4], f // 4 + 1)
            chain = 0

            def link(i):
                nonlocal chain
                chain += 1
                i.then_inc(q["dt_chain"], 1)
                ve.wait_ge(q["dt_chain"], chain)

            link(ve.tensor_scalar(dtm[:, :, :], dtx[:, :, :], -1.0, None, ALU.mult))
            link(ve.tensor_tensor(dtr_[:, :, :], dtm[:, :, :], dtx[:, :, :], ALU.max))
            ve.wait_ge(q["ln_chain"], 2)
            link(ve.tensor_scalar(dtm[:, :, :], dtu[:, :, :], 1.0, None, ALU.add))
            ve.wait_ge(q["ln_chain"], 3)
            link(ve.tensor_scalar(dtm[:, :, :], dtm[:, :, :], -1.0, None, ALU.add))
            link(ve.tensor_scalar(dt[:, :, :], dtm[:, :, :], 0.0, None, ALU.is_equal))
            link(ve.tensor_tensor(dtm[:, :, :], dtm[:, :, :], dt[:, :, :], ALU.add))
            link(ve.tensor_tensor(dtr_[:, :, :], dtr_[:, :, :], dt[:, :, :], ALU.add))
            link(ve.reciprocal(dtm[:, :, :], dtm[:, :, :]))
            link(ve.tensor_tensor(dtr_[:, :, :], dtr_[:, :, :], dtu[:, :, :], ALU.mult))
            link(ve.tensor_tensor(dtr_[:, :, :], dtr_[:, :, :], dtm[:, :, :], ALU.mult))
            link(ve.scalar_tensor_tensor(out=dt[:, :, :], in0=dtx[:, :, :], scalar=0.0, in1=dtr_[:, :, :], op0=ALU.max, op1=ALU.add))
            link(ve.scalar_tensor_tensor(out=dta[:, :, :], in0=dt[:, :, :], scalar=-1.0,
                                         in1=na[:, :].unsqueeze(1).to_broadcast([P, NT, NH]), op0=ALU.mult, op1=ALU.mult))
            ve.memset(ub[:, :, :, 0:CW - 1], 0.0).then_inc(q["u_zero"], 1)
            ve.wait_ge(q["u_zero"], 1)
            ve.memset(stat[:, 0:1], 0.0).then_inc(q["dt_ready"], 1)
            cc = 0
            for j in range(12):
                f = fills["bc"] + j if j < 4 else fills["x"] + j - 4
                ve.wait_ge(drained[f % 4], f // 4 + 1)
                for k in range(2):
                    tile = 16 + 2 * j + k if j < 4 else 2 * (j - 4) + k
                    n = 2 * j + k
                    if n >= 2:
                        ve.wait_ge(q["silu_conv"], n - 1)
                    u = ub[:, j % 2, k, :]
                    w = pc[:, PC_CW + CW * tile:PC_CW + CW * tile + CW]
                    ve.tensor_scalar(cv[:, k, :], u[:, CW - 1:], w[:, CW - 1:CW], pc[:, PC_CB + tile:PC_CB + tile + 1], ALU.mult, ALU.add).then_inc(q["conv_chain"], 1)
                    cc += 1
                    for tap in range(CW - 2, -1, -1):
                        ve.wait_ge(q["conv_chain"], cc)
                        cc += 1
                        i = ve.scalar_tensor_tensor(out=cv[:, k, :], in0=u[:, tap:tap + S], scalar=w[:, tap:tap + 1], in1=cv[:, k, :],
                                                    op0=ALU.mult, op1=ALU.add)
                        if tap:
                            i.then_inc(q["conv_chain"], 1)
                        else:
                            i.then_inc(q["conv_done"], 1)
                            cc -= 1
            for s in range(2 * G):
                c, g = divmod(s, G)
                ve.wait_ge(q["cb_full"], s + 1)
                if s >= 1:
                    ve.wait_ge(q["m_ready"], 2 * s)
                ve.tensor_tensor(cbm[:, :], PB[7][:, 0:P], tri, ALU.mult).then_inc(q["cbm_done"], 1)
                ve.wait_ge(q["cbm_done"], s + 1)
                for half in range(2):
                    n = 2 * s + half
                    ve.wait_ge(q["dec_done"], n + 1)
                    dv = dec[:, n % 2]
                    ve.tensor_tensor(dv, dv, cbm[:, :].unsqueeze(1).to_broadcast([P, 4, P]), ALU.mult).then_inc(q["m_ready"], 1)
                xs = y[:, c, 512 * g:512 * g + 512]
                ve.wait_ge(q["xsD_ready"], s + 1)
                ve.wait_ge(q["yd_full"], s + 1)
                if c == 0:
                    ve.tensor_tensor(xs, xsD[:, :, :].rearrange("p h d -> p (h d)"), PB[s % 4 if False else 2 + s % 2][:, :], ALU.add).then_inc(q["yy_done"], 1)
                else:
                    ve.tensor_tensor(xs, xsD[:, :, :].rearrange("p h d -> p (h d)"), PB[2 + s % 2][:, :], ALU.add).then_inc(q["yo_done"], 1)
                    ve.wait_ge(q["yo_full"], s - G + 1)
                    ve.tensor_tensor(yo[:, :].rearrange("p (h d) -> p h d", h=HPG), PB[6][:, :].rearrange("p (h d) -> p h d", h=HPG),
                                     eac[:, HPG * g:HPG * g + HPG].unsqueeze(2).to_broadcast([P, HPG, PH]), ALU.mult).then_inc(q["yo_done"], 1)
                    ve.wait_ge(q["yo_done"], 2 * (s - G + 1))
                    ve.tensor_tensor(xs, xs, yo[:, :], ALU.add).then_inc(q["yy_done"], 1)
            ve.wait_ge(q["yy_done"], 2 * G)
            for n in range(4):
                for t in range(NT):
                    i = 2 * n + t
                    f = fills["z"] + i
                    ve.wait_ge(drained[f % 4], f // 4 + 1)
                    yv = y[:, t, 512 * n:512 * n + 512]
                    ve.tensor_tensor(yv, yv, zs[:, i % 2, :], ALU.mult).then_inc(q["yg_done"], 1)
            norm_T(R_Y, y, PC_GN, cat, DI, y)
            add_out("out1")
            norm_T(R_F1, x, PC_FFN + 8, hT, D, xn)

            chain = 0

            def rlink(i):
                nonlocal chain
                chain += 1
                i.then_inc(q["rt_chain"], 1)
                ve.wait_ge(q["rt_chain"], chain)

            ve.wait_ge(q["rt_full"], 1)
            rlink(ve.tensor_copy(lg[:, :, :], PB[0][:, 0:16].rearrange("p (t e) -> p t e", t=NT)))
            rlink(ve.tensor_reduce(s8[:, :], lg[:, :, :], AX_X, ALU.max))
            for t in range(NT):
                rlink(ve.tensor_scalar(nv1[:, t, :], lg[:, t, :], s8[:, t:t + 1], None, ALU.subtract))
            for t in range(NT):
                mine = lg[:, t, :].unsqueeze(2).to_broadcast([P, NE, NE])
                other = lg[:, t, :].unsqueeze(1).to_broadcast([P, NE, NE])
                rlink(ve.tensor_tensor(cmp1[:, t], other, mine, ALU.is_gt))
                rlink(ve.tensor_tensor(cmp2[:, t], other, mine, ALU.is_equal))
                rlink(ve.tensor_tensor(cmp2[:, t], cmp2[:, t], con[:, C_LT:C_LT + 64].rearrange("p (e j) -> p e j", e=NE), ALU.mult))
                rlink(ve.tensor_tensor(cmp1[:, t], cmp1[:, t], cmp2[:, t], ALU.add))
                rlink(ve.tensor_reduce(rank[:, t, :], cmp1[:, t], AX_X, ALU.add))
            rlink(ve.tensor_scalar(top[:, :, :], rank[:, :, :], 2.0, None, ALU.is_lt))
            ve.wait_ge(q["rt_exp"], 1)
            rlink(ve.tensor_tensor(pe8[:, :, :], pe8[:, :, :], top[:, :, :], ALU.mult))
            rlink(ve.tensor_reduce(s8[:, :], pe8[:, :, :], AX_X, ALU.add))
            rlink(ve.reciprocal(s8[:, :], s8[:, :]))
            rlink(ve.tensor_tensor(comb[:, :, :], pe8[:, :, :], s8[:, :].unsqueeze(2).to_broadcast([P, NT, NE]), ALU.mult))
            with ve.Fori(1, FFN_TURNS) as turn:
                ve.wait_ge(q["y_drained"], turn)
                ffn_mul(turn)
            for t in range(NT):
                c = 2 * R_FIN + t
                ve.wait_ge(q["rstd_done"], c + 1)
                ve.scalar_tensor_tensor(out=xn[:, t, :], in0=x[:, t, :], scalar=rstd[:, c:c + 1], in1=pr[:, PR_GF:PR_GF + D],
                                        op0=ALU.mult, op1=ALU.mult).then_inc(q["final"], 1)

        @block.tensor
        def _(pe):
            mm = nc.tensor.matmul

            def transposed(r, src, width):
                f = TR_BEFORE[r]
                for t in range(NT):
                    pe.wait_ge(q["xn_done"], 2 * r + t + 1 if r < R_Y else 2 * r + t + 1)
                    for k in range(0, width // P, 4):
                        if f >= 2:
                            pe.wait_ge(q["tr_drained"], f - 1)
                        for i in range(4):
                            last = nc.tensor.transpose(PB[4 + f % 2][:, P * i:P * i + P], src[:, t, P * (k + i):P * (k + i) + P], ident)
                        last.then_inc(q["tr_full"], 1)
                        f += 1

            def bank_free(f):
                if f >= 4:
                    pe.wait_ge(drained[f % 4], f // 4)

            def gemm_a_fill(n, f, actT):
                unit_landed(pe, n)
                bank_free(f)
                w = unit_view(n, "a")
                for c in range(2):
                    for k in range(KD):
                        last = mm(PB[f % 4][:, S * c:S * c + S], w[:, k, P * c:P * c + P], actT[:, k, :], start=k == 0, stop=k == KD - 1)
                last.then_inc(q["units_used"], 1)

            def gemm_b(n, f, kgs, actT, tile0=0):
                for kg in range(kgs):
                    unit_landed(pe, n + kg)
                    w = unit_view(n + kg, "b")
                    for t in range(NT):
                        if kg == 0:
                            bank_free(f + t)
                        for k in range(4):
                            kk = 4 * kg + k
                            last = mm(PB[(f + t) % 4][:, :], actT[:, kk, P * t:P * t + P], w[:, k, :],
                                      start=kk == 0, stop=kk == 4 * kgs - 1)
                    last.then_inc(q["units_used"], 1)

            def memory_kv(layer, n):
                for j in range(4):
                    gemm_a_fill(n + j, fills[f"k{layer}"] + j, memT)
                for j in range(2):
                    gemm_b(n + 4 + 2 * j, fills[f"v{layer}"] + 2 * j, 2, memT)

            def scores(s, swa):
                if s >= 2:
                    pe.wait_ge(q["exp_done"], 2 * (s - 1))
                bank = PB[4 + s % 2]
                if swa:
                    b, hp = divmod(s, 8)
                    w = P if b == 0 else S
                    kv = hp // 4
                    for j in range(2):
                        o = bank[:, S * j:S * j + w]
                        mm(o, antiJ, hankel[:, 2 * hp + j, S - w:S], start=True, stop=False)
                        last = mm(o, qT[:, hp, P * b:P * b + P], kz[:, kv, j, P * b + P - w:P * b + P], start=False, stop=True)
                else:
                    h = s % 4
                    for j in range(NT):
                        for k in range(2):
                            last = mm(bank[:, S * j:S * j + S], xqT[:, 2 * h + k, P * j:P * j + P], memK[:, 2 * h + k, :], start=k == 0, stop=k == 1)
                last.then_inc(q["s_full"], 1)

            def transpose_probs(s, swa):
                nk = 1 if swa and s < 8 else 2
                pe.wait_ge(q["p_ready"], s + 1)
                if s >= 1:
                    pe.wait_ge(q["pT_ready"], s)
                for k in range(nk):
                    for j in range(2):
                        last = nc.tensor.transpose(PB[6][:, P * (2 * k + j):P * (2 * k + j) + P], prob[:, s % 2, j, P * k:P * k + P], ident)
                last.then_inc(q["t_full"], 1)

            def values(s, swa):
                pe.wait_ge(q["pT_ready"], s + 1)
                if s >= 1:
                    pe.wait_ge(q["cat_done"], s)
                pt = probT[:, s % 2, :]
                if swa:
                    b, hp = divmod(s, 8)
                    nk = 1 if b == 0 else 2
                    kv = hp // 4
                    for k in range(nk):
                        t = b - nk + 1 + k
                        for j in range(2):
                            last = mm(PB[7][:, 0:P], vz[:, t, kv, 64 - 64 * j:192 - 64 * j], pt[:, P * (2 * k + j):P * (2 * k + j) + P],
                                      start=k == 0 and j == 0, stop=k == nk - 1 and j == 1)
                else:
                    h = s % 4
                    for d in range(2):
                        for k in range(2):
                            last = mm(PB[7][:, S * d:S * d + S], memV[:, k, XD * h + P * d:XD * h + P * d + P], pt[:, S * k:S * k + S],
                                      start=k == 0, stop=k == 1)
                last.then_inc(q["o_full"], 1)

            def softmax_steps(first, last, swa):
                scores(first, swa)
                for s in range(first, last):
                    if s + 1 < last:
                        scores(s + 1, swa)
                    if s > first:
                        values(s - 1, swa)
                    transpose_probs(s, swa)
                values(last - 1, swa)

            def ffn(u, turn):
                first = isinstance(turn, int)
                t33 = ffn_turn(turn)[1]

                def down(c):
                    n = u + ffn_at(c, 2)
                    unit_landed(pe, n, t33)
                    pe.wait_ge(q["act_done"], c + 1 + turn * FC)
                    if c == 0 and not first:
                        pe.wait_ge(q["y_drained"], turn)
                    w = unit_view(n, "d")
                    for t in range(NT):
                        for nn in range(2):
                            for k in range(2):
                                last = mm(PB[4 + 2 * nn + t][:, :], act[:, c % 2, k, P * t:P * t + P], w[:, k, 512 * nn:512 * nn + 512],
                                          start=c == 0 and k == 0, stop=c == FC - 1 and k == 1)
                    last.then_inc(q["units_used"], 1)

                for c in range(FC):
                    for half in range(2):
                        n = u + ffn_at(c, half)
                        unit_landed(pe, n, t33)
                        if c >= 2:
                            pe.wait_ge(q["act_done"], c - 1 + turn * FC)
                        elif not first:
                            pe.wait_ge(q["act_done"], turn * FC)
                        w = unit_view(n, "a")
                        for cc in range(2):
                            for k in range(KD):
                                last = mm(PB[2 * (c % 2) + half][:, S * cc:S * cc + S], w[:, k, P * cc:P * cc + P], hT[:, k, :],
                                          start=k == 0, stop=k == KD - 1)
                        last.then_inc(q["units_used"], 1)
                    if c:
                        down(c - 1)
                down(FC - 1)

            pe.wait_ge(q["par_in"], 48)
            transposed(R_MEM0, xn, D)
            pe.wait_ge(q["rel_in"], 32)
            mm(PB[6][0:HQ, 0:P], rel[:, :], buck[:, :], start=True, stop=True).then_inc(q["bias_full"], 1)
            transposed(R_H0, xn, D)
            pe.wait_ge(q["tr_drained"], 4)
            memory_kv(0, 0)
            pe.wait_ge(q["tr_drained"], 8)
            n = 8
            for j in range(4):
                gemm_a_fill(n + j, fills["q"] + j, hT)
            n, f = 12, fills["kv"]
            unit_landed(pe, n)
            bank_free(f)
            w = unit_view(n, "a")
            for k in range(KD):
                mm(PB[f % 4][:, 0:S], w[:, k, 0:P], hT[:, k, :], start=k == 0, stop=k == KD - 1)
            for t in range(NT):
                for k in range(KD):
                    last = mm(PB[f % 4][:, S + P * t:S + P * t + P], hT[:, k, P * t:P * t + P], w[:, k, P:2 * P], start=k == 0, stop=k == KD - 1)
            last.then_inc(q["units_used"], 1)
            n = 13
            for j in range(4):
                gemm_a_fill(n + j, fills["xq0"] + j, hT)
            pe.wait_ge(q["hank_in"], 16)
            pe.wait_ge(drained[fills["kv"] % 4], fills["kv"] // 4 + 1)
            pe.wait_ge(q["qk_ready"], 5)
            softmax_steps(0, 16, True)
            fills_drained(pe, "xq0")
            softmax_steps(16, 20, False)
            pe.wait_ge(q["cat_done"], 20)
            for j in range(2):
                gemm_b(17 + 4 * j, fills["out0"] + 2 * j, 4, cat)
            transposed(R_F0, xn, D)
            pe.wait_ge(q["tr_drained"], 12)
            ffn(FFN0, 0)

            pe.wait_ge(q["y_drained"], 1)
            transposed(R_MEM1, xn, D)
            transposed(R_H1, xn, D)
            pe.wait_ge(q["tr_drained"], 20)
            memory_kv(1, L1)
            for j in range(4):
                gemm_a_fill(L1 + 8 + j, fills["xq1"] + j, hT)
            fills_drained(pe, "xq1")
            softmax_steps(20, 24, False)
            n, f = L1 + 12, fills["dt"]
            unit_landed(pe, n)
            bank_free(f)
            w = unit_view(n, "t")
            for t in range(NT):
                for k in range(KD):
                    last = mm(PB[f % 4][:, NH * t:NH * t + NH], hT[:, k, P * t:P * t + P], w[:, k, :], start=k == 0, stop=k == KD - 1)
            last.then_inc(q["units_used"], 1)
            for j in range(2):
                gemm_a_fill(L1 + 13 + j, fills["bc"] + j, hT)
            pe.wait_ge(q["dt_ready"], 1)
            mm(PB[4][:, 0:NH], tri, dta[:, 1, :], start=True, stop=True)
            mm(PB[4][:, 64:64 + NH], su, dta[:, 0, :], start=True, stop=True).then_inc(q["dta_full"], 1)
            for j in range(2, 4):
                gemm_a_fill(L1 + 13 + j, fills["bc"] + j, hT)

            def x_transposes(j):
                pe.wait_ge(q["silu_conv"], 2 * j + 10)
                if j >= 1:
                    pe.wait_ge(q["xs_ready"], j)
                for t in range(NT):
                    for k in range(2):
                        last = nc.tensor.transpose(PB[6][:, S * t + P * k:S * t + P * k + P], xcT[:, j % 2, k, P * t:P * t + P], ident)
                last.then_inc(q["xT_full"], 1)

            for j in range(8):
                gemm_a_fill(L1 + 17 + j, fills["x"] + j, hT)
                if j >= 1:
                    x_transposes(j - 1)
            x_transposes(7)
            for s in range(2 * G):
                c, g = divmod(s, G)
                BT, CT = BCT[:, g, P * c:P * c + P], BCT[:, G + g, P * c:P * c + P]
                if s == 0:
                    pe.wait_ge(q["eac_done"], 2)
                    pe.wait_ge(q["silu_conv"], 24)
                    fills_drained(pe, "x")
                if s >= 1:
                    pe.wait_ge(q["cbm_done"], s)
                if s >= 1 and s <= G:
                    pe.wait_ge(q["btok_done"], s)
                last = mm(PB[7][:, 0:P], BT, CT, start=True, stop=True)
                last.then_inc(q["cb_full"], 1)
                if c == 0:
                    pe.wait_ge(q["cbm_done"], s + 1)
                    nc.tensor.transpose(PB[7][:, 256:384], BT, ident).then_inc(q["bt_full"], 1)
                for half in range(2):
                    n = 2 * s + half
                    pe.wait_ge(q["l_ready"], n + 1)
                    if n >= 2:
                        pe.wait_ge(q["dec_done"], n - 1)
                    for h in range(4):
                        last = mm(PB[4 + n % 2][:, P * h:P * h + P], Lm[:, n % 2, h, :], tri, start=True, stop=True)
                    last.then_inc(q["seg_full"], 1)
                if c == 0:
                    pe.wait_ge(q["btok_done"], s + 1)
                    pe.wait_ge(q["xde_ready"], s + 1)
                    if s >= 1:
                        pe.wait_ge(q["st_done"], s)
                    mm(PB[6][:, :], btok[:, :], xde[:, :, :].rearrange("p h d -> p (h d)"), start=True, stop=True).then_inc(q["st_full"], 1)
                else:
                    pe.wait_ge(q["st_done"], G)
                    if s > G:
                        pe.wait_ge(q["yo_done"], 2 * (s - G))
                    mm(PB[6][:, :], CT, st[:, g, :], start=True, stop=True).then_inc(q["yo_full"], 1)
                pe.wait_ge(q["xdt_ready"], s + 1)
                if s >= 2:
                    pe.wait_ge(q["yy_done"], s - 1)
                for h in range(HPG):
                    n = 2 * s + h // 4
                    pe.wait_ge(q["m_ready"], n + 1)
                    last = mm(PB[2 + s % 2][:, PH * h:PH * h + PH], dec[:, n % 2, h % 4, :], xdt[:, h, :], start=True, stop=True)
                last.then_inc(q["yd_full"], 1)
            pe.wait_ge(q["yy_done"], 2 * G)
            for j in range(4):
                gemm_b(L1 + 25 + 2 * j, fills["z"] + 2 * j, 2, hT)
            transposed(R_Y, y, DI)
            pe.wait_ge(q["tr_drained"], 28)
            pe.wait_ge(q["cat_done"], 24)
            for j in range(2):
                gemm_b(L1 + 33 + 6 * j, fills["out1"] + 2 * j, 6, cat)
            transposed(R_F1, xn, D)
            pe.wait_ge(q["tr_drained"], 32)
            for t in range(NT):
                for k in range(KD):
                    last = mm(PB[0][:, NE * t:NE * t + NE], hT[:, k, P * t:P * t + P], pc[:, PC_RT + NE * k:PC_RT + NE * k + NE],
                              start=k == 0, stop=k == KD - 1)
            last.then_inc(q["rt_full"], 1)
            pe.wait_ge(q["rt_chain"], 1)
            with pe.Fori(1, FFN_TURNS) as turn:
                ffn(MOE, turn)


_NAMES = ["x", "mem", "w_mem_kv", "rel_bias", "swa_w_in", "swa_w_out", "ssm_w_in", "ssm_w_out",
          "ffn_w_gate", "ffn_w_up", "ffn_w_down", "moe_w_gate", "moe_w_up", "moe_w_down"]


def kernel(**inputs):
    import numpy as _np
    import concourse.bacc as _bacc
    from concourse.bass_utils import run_bass_kernel_spmd as _run

    i = {k: _np.ascontiguousarray(v) for k, v in inputs.items()}

    def tiles(v):
        return v.reshape(-1, P).T

    arrays = {n: i[n] for n in _NAMES}
    arrays["pcol"] = _np.ascontiguousarray(_np.concatenate(
        [tiles(i[g][layer]) for g in ("g_mix", "g_ffn", "g_mem") for layer in range(2)]
        + [i["ssm_conv_w"][0].reshape(CW, 24, P).transpose(2, 1, 0).reshape(P, 24 * CW)]
        + [tiles(i["ssm_conv_b"][0]), tiles(i["ssm_g_norm"][0])]
        + [i["moe_w_router"][0].reshape(KD, P, NE).transpose(1, 0, 2).reshape(P, KD * NE)], axis=1))
    arrays["prow"] = _np.ascontiguousarray(_np.concatenate(
        [i["swa_sinks"][0], i["ssm_dt_bias"][0], i["ssm_A_log"][0], i["ssm_D"][0], i["g_final"]])[None, :])
    arrays["const"] = constants()
    arrays["bucket"] = bucket_rows()
    nc = _bacc.Bacc("TRN2", target_bir_lowering=False, num_devices=1)
    aps = {n: nc.dram_tensor(f"in_{n}", v.shape, F32, kind="ExternalInput").ap() for n, v in arrays.items()}
    out = nc.dram_tensor("out_0", (1, S, D), F32, kind="ExternalOutput").ap()
    trunk(nc, aps, out)
    r = _run(nc, [{f"in_{n}": v for n, v in arrays.items()}], core_ids=[0])
    return r.results[0]["out_0"]
```

```python
import math
from contextlib import ExitStack

import numpy as np

import concourse.bass as bass
from concourse import mybir

F32 = mybir.dt.float32
F32R = mybir.dt.float32r
I32 = mybir.dt.int32
ALU = mybir.AluOpType
ACT = mybir.ActivationFunctionType
AX_X = mybir.AxisListType.X

P = 128
D = 1024
KD = D // P
NT = 2
S = NT * P
EPS = 1e-6
NEG = -1e30

HQ, HD = 16, 64
NB, MAX_DIST = 32, 128
HX, XD = 4, 256
DI = 2048
KI = DI // P
NH = 32
G, HPG, PH = 4, 8, 64
KBC = 8
CW = 4
FF = 2816
NE = 8
FC = FF // 256

PC_MIX, PC_FFN, PC_MEM = 0, 16, 32
PC_CW = 48
PC_CB = PC_CW + 24 * CW
PC_GN = PC_CB + 24
PC_RT = PC_GN + KI
PC_N = PC_RT + KD * NE
PR_SINK, PR_DTB, PR_ALOG, PR_D, PR_N = 0, 16, 48, 80, 112
C_ID, C_TRI, C_SU, C_J, C_ONE, C_IO, C_ST, C_LT, C_E, C_K, C_N = 0, 128, 256, 384, 512, 640, 768, 896, 960, 968, 992

RING = 3
HIS, LOS = 3, 2
ES = 5
GATHER_BANK = (7, 0, 1, 7)
FCJ = 6
UJ = 33
SLOTS = P
OVER = 3
SLOT_GROUPS = (ES, ES, ES - 1, ES, ES - 1, ES, ES)
assert sum(SLOT_GROUPS) == UJ
UNIT = 2048


def constants():
    c = np.zeros((P, C_N), np.float32)
    i, j = np.arange(P)[:, None], np.arange(P)[None, :]
    c[:, C_ID:C_ID + P] = i == j
    c[:, C_TRI:C_TRI + P] = i <= j
    c[:, C_SU:C_SU + P] = i > j
    c[:, C_J:C_J + P] = i + j == P - 1
    c[:, C_ONE:C_ONE + P] = 1.0
    e = np.arange(NE)
    c[:, C_IO:C_IO + P] = j
    c[:, C_ST:C_ST + P] = i < j
    c[:, C_E:C_E + NE] = e
    c[:, C_K:C_K + OVER * NE] = np.repeat(np.arange(OVER), NE)
    c[:, C_LT:C_LT + 64] = (e[None, :] < e[:, None]).astype(np.float32).reshape(1, 64)
    return c


def bucket_rows():
    d = np.arange(P - 1, -1, -1)
    half = NB // 2
    far = half + (np.log(np.maximum(d, 1).astype(np.float32) / np.float32(half)) / np.float32(math.log(MAX_DIST / half))
                  * np.float32(NB - half)).astype(np.int32)
    b = np.where(d < half, d, np.minimum(far, NB - 1))
    return (np.arange(NB)[:, None] == b[None, :]).astype(np.float32)


def weight_units(a):
    def cols(w, c0, n):
        return w.rearrange("(t p) n -> p t n", p=P)[:, :, c0:c0 + n]

    def kb(w, kg, n):
        return w.rearrange("(t p) n -> p t n", p=P)[:, 4 * kg:4 * kg + 4, 512 * n:512 * n + 512]

    units = []
    for layer in range(2):
        if layer == 1:
            units += [(kb(a["swa_w_out"][0], kg, n), "b") for n in range(2) for kg in range(4)]
        mk = a["w_mem_kv"][layer]
        units += [(cols(mk, 256 * j, 256), "a") for j in range(4)]
        units += [(kb(mk, kg, 2 + n), "b") for n in range(2) for kg in range(2)]
        if layer == 0:
            units += [(cols(a["swa_w_in"][0], 256 * j, 256), "a") for j in range(9)]
    ffn = [None] * (3 * FC)
    for c in range(FC):
        ffn[ffn_at(c, 0)] = (cols(a["ffn_w_gate"][0], 256 * c, 256), "a")
        ffn[ffn_at(c, 1)] = (cols(a["ffn_w_up"][0], 256 * c, 256), "a")
        ffn[ffn_at(c, 2)] = (a["ffn_w_down"][0].rearrange("(t p) n -> p t n", p=P)[:, 2 * c:2 * c + 2, :], "d")
    units += ffn
    w = a["ssm_w_in"][0]
    units += [(cols(w, DI + 3072 + NH + 256 * j, 256), "a") for j in range(4)]
    units += [(cols(w, DI + 3072, NH), "t")]
    units += [(cols(w, 2 * DI + 256 * j, 256), "a") for j in range(4)]
    units += [(cols(w, DI + 256 * j, 256), "a") for j in range(8)]
    units += [(kb(w, kg, n), "b") for n in range(4) for kg in range(2)]
    units += [(kb(a["ssm_w_out"][0], kg, n), "b") for n in range(2) for kg in range(6)]
    return units


def ffn_at(c, part):
    if part == 2:
        return 3 * c + 4 if c < FC - 1 else 3 * FC - 1
    return max(3 * c - 1, 0) + part


def job_unit(c, part):
    gate = 0 if c == 0 else 4 + 6 * (c - 1)
    if part == 2:
        return UJ - 1 if c == FCJ - 1 else 30 if c == FCJ - 2 else 8 + 6 * c
    return gate + part * (1 if c == FCJ - 1 else 2)


def slot(m):
    for g in SLOT_GROUPS:
        if m < g:
            return m
        m -= g


def slot_before(m):
    return max(u for u in range(-UJ, m) if slot(u % UJ) == slot(m))


def slot_uses(i, m):
    return sum(1 for u in range(m) if slot(u) == i)


def trunk(nc, a, out):
    units = weight_units(a)
    OUT0, KV1, FFN0, L1, MOE = 17, 25, 33, 33 + 3 * FC, len(units)

    ctx = ExitStack()
    with ctx:
        def sb(name, shape, dtype=F32, stack=ctx):
            return stack.enter_context(nc.sbuf_tensor(name, shape, dtype))

        def sem(name):
            return ctx.enter_context(nc.semaphore(name))

        ring = sb("ring", [P, RING, UNIT])
        whi = sb("whi", [P, HIS, UNIT], F32R)
        wlo = sb("wlo", [P, LOS, UNIT], F32R)
        x = sb("x", [P, NT, D])
        hT_hi, hT_lo = sb("hT_hi", [P, KD, S], F32R), sb("hT_lo", [P, KD, S], F32R)
        cat_hi, cat_lo = sb("cat_hi", [P, 24, S], F32R), sb("cat_lo", [P, 24, S], F32R)
        nt = sb("nt", [P, 2, 512])
        actf = sb("actf", [P, 2, 512])
        with ExitStack() as early:
            memK = sb("memK", [P, KD, S], F32, early)
            memV = sb("memV", [P, NT, D], F32, early)
            xqT = sb("xqT", [P, KD, S], F32, early)
        with ExitStack() as late:
            y = sb("y", [P, NT, DI], F32, late)
            with ExitStack() as scan:
                st = sb("st", [P, G, 512], F32, scan)
            st_hi = sb("st_hi", [P, UNIT], F32R, late)
        sb("pair_a", [P, 6 * D])
        with ExitStack() as early:
            mem = sb("mem", [P, NT, D], F32, early)
        with ExitStack() as late:
            prob = sb("prob", [P, 2, 2, S], F32, late)
            probT = sb("probT", [P, 2, 2 * S], F32, late)
        with ExitStack() as end:
            gfin = sb("gfin", [P, D], F32, end)
            grow = sb("grow", [P, D], F32, end)
        sb("pair_b", [P, 2 * D])
        with ExitStack() as l0:
            xn = sb("xn", [P, NT, D], F32, l0)
        with ExitStack() as experts:
            xn_lo = sb("xn_lo", [P, UNIT], F32R, experts)
        with ExitStack() as l0:
            qT = sb("qT", [P, KD, S], F32, l0)
        with ExitStack() as l1:
            BCT = sb("BCT", [P, KBC, S], F32, l1)
        sb("pair_c", [P, 2 * D])
        with ExitStack() as l0:
            kz = sb("kz", [P, 2, 2, S], F32, l0)
            vz = sb("vz", [P, NT, 2, 192], F32, l0)
        with ExitStack() as l1:
            with ExitStack() as conv:
                ub = sb("ub", [P, 2, 2, S + CW - 1], F32, conv)
                cv = sb("cv", [P, 2, S], F32, conv)
                xcT = sb("xcT", [P, 2, 2, S], F32, conv)
            with ExitStack() as scan:
                zs = sb("zs", [P, 2, 512], F32, scan)
                yo = sb("yo", [P, 512], F32, scan)
                xde = sb("xde", [P, HPG, PH], F32, scan)
                xsD = sb("xsD", [P, HPG, PH], F32, scan)
            sb("pair_d", [P, 2600], F32, l1)
            dtx, dtu, dtr_, dtm, dt, dta = (sb(n, [P, NT, NH], F32, l1) for n in ("dtx", "dtu", "dtr", "dtm", "dt", "dta"))
            cbm = sb("cbm", [P, P], F32, l1)
            btok = sb("btok", [P, P], F32, l1)
            xdt = sb("xdt", [P, HPG, PH], F32, l1)
        with ExitStack() as moe:
            cmp1, cmp2 = sb("cmp1", [P, NT, NE, NE], F32, moe), sb("cmp2", [P, NT, NE, NE], F32, moe)
            lg, rank, top, nv1, pe8, comb, posm = (sb(n, [P, NT, NE], F32, moe) for n in ("lg", "rank", "top", "nv1", "pe8", "comb", "posm"))
            s8 = sb("s8", [P, NT], F32, moe)
            full, before = sb("full", [P, NE], F32, moe), sb("before", [P, NE], F32, moe)
            oh, pick = sb("oh", [P, OVER, NE], F32, moe), sb("pick", [P, OVER, NE], F32, moe)
            jobpos = sb("jobpos", [P, NT, NE + OVER], F32, moe)
            jobcomb = sb("jobcomb", [P, NT, 1 + NE + OVER], F32, moe)
            overe, jobs = sb("overe", [P, OVER], F32, moe), sb("jobs", [P, 1], F32, moe)
            overe_i, jobs_i = sb("overe_i", [P, OVER], I32, moe), sb("jobs_i", [P, 1], I32, moe)
            elo3 = sb("elo3", [P, UNIT], F32R, moe)
        sb("pair_e", [P, 2600 + 6 * NT * NH + 2 * P + 512])
        Lm = actf[:, :, :].rearrange("p a (h t) -> p a h t", h=4)
        dec = nt[:, :, :].rearrange("p a (h t) -> p a h t", h=4)
        con = sb("con", [P, C_N])
        pc = sb("pc", [P, PC_N])
        pr = sb("pr", [P, PR_N])
        ssq, var, rstd = sb("ssq", [P, 16]), sb("var", [P, 16]), sb("rstd", [P, 16])
        mhalf = sb("mhalf", [P, 1])
        stat = sb("stat", [P, 1])
        nsink = sb("nsink", [P, HQ])
        mx, nm, sd, es, sm, den, rden = (sb(n, [P, 2, 2]) for n in ("mx", "nm", "sd", "es", "sm", "den", "rden"))
        na = sb("na", [P, NH])
        eac, toe = sb("eac", [P, NH]), sb("toe", [P, NH])
        rel = sb("rel", [NB, HQ])
        buck = sb("buck", [NB, P])
        brow = sb("brow", [HQ, 384])
        brow_dram = nc.dram_tensor("brow_dram", (HQ, 384), F32, kind="Internal").ap()

        memT_hi, memT_lo = cat_hi[:, 0:KD, :], cat_lo[:, 0:KD, :]
        act_hi, act_lo = (c[:, 8:12, :].rearrange("p (a k) s -> p a k s", a=2) for c in (cat_hi, cat_lo))
        hn_hi, hn_lo = (c[:, 0:8, :].rearrange("p (t k) s -> p t (k s)", t=NT) for c in (cat_hi, cat_lo))
        xg_hi, xg_lo = (c[:, 8:12, :].rearrange("p a (b s) -> p (a b) s", b=2) for c in (cat_hi, cat_lo))
        aT_hi, aT_lo = (c[:, 12:16, :].rearrange("p (a k) (b s) -> p a (k b) s", a=2, b=2) for c in (cat_hi, cat_lo))
        y_hi, y_lo = (c[:, 16:20, :].rearrange("p a s -> p (a s)") for c in (cat_hi, cat_lo))
        sel = cat_hi[:, 20, :].rearrange("p (t s) -> p t s", t=NT)
        selT = cat_hi[:, 21, :].rearrange("p (t s) -> p t s", t=NT)
        memT1_hi, memT1_lo = cat_hi[:, 16:24, :], cat_lo[:, 16:24, :]
        hankel = [c[:, 16:24, :] for c in (cat_hi, cat_lo)]
        hTf = st[:, :, :].rearrange("p g (a s) -> p (g a) s", a=2)
        eraw = [ring[:, (MOE + i) % RING, :] for i in range(RING)] + [y[:, t, :] for t in range(NT)]
        ehi = [whi[:, (MOE + i) % HIS, :] for i in range(HIS)] + [hT_hi[:, :, :].rearrange("p k s -> p (k s)"), st_hi[:, :]]
        elo = [wlo[:, i, :] for i in range(LOS)] + [hT_lo[:, :, :].rearrange("p k s -> p (k s)"), elo3[:, :], xn_lo[:, :]]

        PB = [ctx.enter_context(nc.psum_tensor(f"PB{i}", [P, 512], F32)) for i in range(8)]
        names = """x_in mem_in par_in rel_in brow_set brow_st hank_in stores units_used mhalf_set nsink_set bias_full brow_done
            kz_zero sq_done var_done rstd_done xn_done tr_full tr_drained s_full mx_done nm_done sd_done exp_done es_done
            den_done rden_done p_ready t_full pT_ready o_full cat_done qk_ready silu_done act_done y_drained dt_chain
            dt_ready ln_chain dta_full eac_done u_zero conv_chain conv_done silu_conv xT_full xs_ready hi_ready lo_ready
            t_hi t_lo cat_hi_done a_hi a_lo late_in lg_full top_done pos_full jobs_ready hn_mul hn_ready sel_ready
            selT_full selT_done ga_full ga_done e_silu e_act e_t e_thi e_tlo yhi_done ylo_done sc_full sc_done cb_full
            cbm_done l_ready seg_full dec_done m_ready bt_full btok_done st_full st_done xdt_ready xde_ready xsD_ready
            yd_full yo_full yo_done yy_done yg_done rt_chain rt_exp final""".split()
        q = {n: sem(n) for n in names}
        raw_in = [sem(f"raw_in{i}") for i in range(RING)]
        expert_in = [sem(f"expert_in{i}") for i in range(ES)]
        drained = [sem(f"drained{i}") for i in range(4)]

        ident = con[:, C_ID:C_ID + P]
        tri = con[:, C_TRI:C_TRI + P]
        su = con[:, C_SU:C_SU + P]
        antiJ = con[:, C_J:C_J + P]
        block = ctx.enter_context(nc.Block())

        def unit_view(n, kind):
            r = ring[:, n % RING, :]
            if kind == "a":
                return r.rearrange("p (k c) -> p k c", k=8)
            if kind == "b":
                return r.rearrange("p (k c) -> p k c", k=4)
            if kind == "d":
                return r.rearrange("p (k c) -> p k c", k=2)
            return r[:, 0:8 * NH].rearrange("p (k c) -> p k c", k=8)

        def parts(n, kind):
            k = {"a": 8, "b": 4, "d": 2, "t": 8}[kind]
            w = 8 * NH if kind == "t" else UNIT
            pair = (whi[:, n % HIS, 0:w], wlo[:, n % LOS, 0:w]) if n < MOE else (ehi[slot(n - MOE)], elo[slot(n - MOE)])
            return tuple(v.rearrange("p (k c) -> p k c", k=k) for v in pair)

        def width(n):
            return 8 * NH if n == L1 + 4 else UNIT

        def unit_landed(eng, n):
            eng.wait_ge(raw_in[n % RING], 16 * (n // RING + 1))

        def expert_landed(eng, m, job):
            i = slot(m)
            eng.wait_ge(expert_in[i], 16 * (slot_uses(i, m) + 1) + job * (16 * slot_uses(i, UJ)))

        R_MEM0, R_H0, R_MEM1, R_F0, R_H1, R_Y, R_F1, R_FIN = range(8)
        TR_BEFORE = {R_MEM0: 0, R_H0: 4, R_MEM1: 8, R_F0: 12, R_H1: 16, R_Y: 20, R_F1: 28}

        fills, last_unit = {}, []
        for name, start, n, per in (("k0", 0, 4, 1), ("v0", 4, 4, 2), ("q", 8, 4, 1), ("kv", 12, 1, 1), ("xq0", 13, 4, 1),
                                    ("out0", OUT0, 4, 4), ("k1", KV1, 4, 1), ("v1", KV1 + 4, 4, 2), ("xq1", L1, 4, 1), ("dt", L1 + 4, 1, 1),
                                    ("bc", L1 + 5, 4, 1), ("x", L1 + 9, 8, 1), ("z", L1 + 17, 8, 2), ("out1", L1 + 25, 4, 6)):
            fills[name] = len(last_unit)
            last_unit += [start + j if per == 1 else start + per * (j // NT) + per - 1 for j in range(n)]

        def fill_ready(eng, f):
            eng.wait_ge(q["units_used"], last_unit[f] + 1)

        def fills_drained(eng, name):
            end = fills[name] + {"out0": 4, "out1": 4, "xq0": 4, "xq1": 4, "v1": 4, "x": 8}[name]
            for f in range(end - 4, end):
                eng.wait_ge(drained[f % 4], f // 4 + 1)

        @block.sync
        def _(sp):
            sp.dma_start(mem[:, :, :], a["mem"][0].rearrange("(t p) d -> p t d", p=P)).then_inc(q["mem_in"], 16)
            sp.dma_start(pc[:, :], a["pcol"]).then_inc(q["par_in"], 16)
            sp.dma_start(con[:, :], a["const"]).then_inc(q["par_in"], 16)
            sp.dma_start(pr[:, :], a["prow"].partition_broadcast(P).rearrange("p a n -> p (a n)")).then_inc(q["par_in"], 16)
            sp.dma_start(x[:, :, :], a["x"][0].rearrange("(t p) d -> p t d", p=P)).then_inc(q["x_in"], 16)

            def load(n):
                if n >= RING:
                    sp.wait_ge(q["lo_ready"], n - RING + 1)
                src, kind = units[n]
                sp.dma_start(unit_view(n, kind), src).then_inc(raw_in[n % RING], 16)

            for n in range(RING):
                load(n)
            sp.dma_start(rel[:, :], a["rel_bias"]).then_inc(q["rel_in"], 16)
            sp.dma_start(buck[:, :], a["bucket"]).then_inc(q["rel_in"], 16)
            sp.wait_ge(q["brow_done"], 1)
            sp.dma_start(brow_dram, brow[:, :]).then_inc(q["brow_st"], 16)
            sp.wait_ge(q["brow_st"], 16)
            for half in range(2):
                sp.dma_start(hankel[half].bitcast(F32), bass.AP(brow_dram.tensor, 384 * 8 * half, [[1, P], [384, 8], [1, S]])).then_inc(q["hank_in"], 16)
            for n in range(RING, OUT0 + RING):
                load(n)
            sp.wait_ge(q["s_full"], 16)
            sp.dma_start(xn[:, :, :], a["mem"][0].rearrange("(t p) d -> p t d", p=P)).then_inc(q["mem_in"], 16)
            for n in range(OUT0 + RING, MOE):
                load(n)
            sp.wait_ge(q["cat_done"], 24)
            sp.dma_start(grow[:, :], a["g_ffn"][1:2, :].partition_broadcast(P).rearrange("p a n -> p (a n)")).then_inc(q["late_in"], 16)
            sp.dma_start(gfin[:, :], a["g_final"].partition_broadcast(P).rearrange("p a n -> p (a n)")).then_inc(q["late_in"], 16)

            sp.wait_ge(q["tr_full"], 28)
            sp.wait_ge(q["lo_ready"], MOE)

            def expert_loads(job, e):
                def w(name):
                    return a[name][0, bass.ds(e, 1)].rearrange("e (t p) n -> p (e t) n", p=P)
                srcs = [None] * UJ
                for part, name in enumerate(("moe_w_gate", "moe_w_up")):
                    for c in range(FCJ - 1):
                        for kg in range(2):
                            srcs[job_unit(c, part) + kg] = (w(name)[:, 4 * kg:4 * kg + 4, 512 * c:512 * c + 512], "b")
                    srcs[job_unit(FCJ - 1, part)] = (w(name)[:, :, 512 * (FCJ - 1):FF], "a")
                for c in range(FCJ - 1):
                    for n in range(2):
                        srcs[job_unit(c, 2) + n] = (w("moe_w_down")[:, 4 * c:4 * c + 4, 512 * n:512 * n + 512], "b")
                srcs[job_unit(FCJ - 1, 2)] = (w("moe_w_down")[:, 20:22, :], "d")
                for m, (src, kind) in enumerate(srcs):
                    k = {"a": 8, "b": 4, "d": 2}[kind]
                    sp.wait_ge(q["lo_ready"], MOE + slot_before(m) + 1 + job * UJ)
                    sp.dma_start(eraw[slot(m)].rearrange("p (k c) -> p k c", k=k), src).then_inc(expert_in[slot(m)], 16)

            with sp.Fori(0, NE) as e:
                expert_loads(e, e)
            sp.wait_ge(q["jobs_ready"], 1)
            last = sp.value_load(jobs_i[0:1, 0:1], min_val=NE - 1, max_val=NE - 1 + OVER)
            with sp.If(last > NE - 1):
                with sp.Fori(NE, last + 1) as job:
                    expert_loads(job, sp.value_load(overe_i[0:1, bass.ds(job - NE, 1)], min_val=0, max_val=NE - 1))
            sp.wait_ge(q["final"], 2)
            sp.dma_start(out[0].rearrange("(t p) d -> p t d", p=P), xn[:, :, :]).then_inc(q["stores"], 16)
            sp.wait_ge(q["stores"], 16)

        @block.gpsimd
        def _(pool):
            pool.memset(mhalf[:, :], -0.5).then_inc(q["mhalf_set"], 1)
            pool.memset(kz[:, :, :, :], 0.0).then_inc(q["kz_zero"], 1)
            pool.memset(vz[:, :, :, :], 0.0).then_inc(q["kz_zero"], 1)
            pool.wait_ge(q["mhalf_set"], 1)

            def rms(r, width):
                for t in range(NT):
                    c = 2 * r + t
                    pool.wait_ge(q["sq_done"], c + 1)
                    pool.tensor_scalar(var[:, c:c + 1], ssq[:, c:c + 1], 1.0 / width, EPS, ALU.mult, ALU.add).then_inc(q["var_done"], 1)
                    pool.wait_ge(q["var_done"], c + 1)
                    pool.tensor_tensor(rstd[:, c:c + 1], var[:, c:c + 1], mhalf[:, :], ALU.pow).then_inc(q["rstd_done"], 1)

            for r in (R_MEM0, R_H0, R_MEM1, R_F0, R_H1):
                rms(r, D)

            pool.wait_ge(q["dt_ready"], 1)
            pool.wait_ge(q["par_in"], 48)
            for s in range(2 * G):
                c, g = divmod(s, G)
                xs = y[:, c, 512 * g:512 * g + 512].rearrange("p (h d) -> p h d", h=HPG)
                for half in range(2):
                    h0 = HPG * g + 4 * half
                    n = 2 * s + half
                    if n >= 2:
                        pool.wait_ge(q["seg_full"], n - 1)
                    pool.tensor_tensor(Lm[:, n % 2], su.unsqueeze(1).to_broadcast([P, 4, P]),
                                       dta[:, c, h0:h0 + 4].unsqueeze(2).to_broadcast([P, 4, P]), ALU.mult).then_inc(q["l_ready"], 1)
                if s == 0:
                    pool.wait_ge(q["xs_ready"], 8)
                    pool.wait_ge(q["eac_done"], 2)
                if s >= 1:
                    pool.wait_ge(q["yd_full"], s)
                pool.tensor_tensor(xdt[:, :, :], xs, dt[:, c, HPG * g:HPG * g + HPG].unsqueeze(2).to_broadcast([P, HPG, PH]),
                                   ALU.mult).then_inc(q["xdt_ready"], 1)
                if c == 0:
                    pool.wait_ge(q["xdt_ready"], s + 1)
                    if s >= 1:
                        pool.wait_ge(q["st_full"], s)
                    pool.tensor_tensor(xde[:, :, :], xdt[:, :, :], toe[:, HPG * g:HPG * g + HPG].unsqueeze(2).to_broadcast([P, HPG, PH]),
                                       ALU.mult).then_inc(q["xde_ready"], 1)
                if s >= 1:
                    pool.wait_ge(q["yy_done"], s)
                pool.tensor_tensor(xsD[:, :, :], xs, pr[:, PR_D + HPG * g:PR_D + HPG * g + HPG].unsqueeze(2).to_broadcast([P, HPG, PH]),
                                   ALU.mult).then_inc(q["xsD_ready"], 1)
            rms(R_Y, DI)
            rms(R_F1, D)
            rms(R_FIN, D)

        @block.scalar
        def _(ac):
            split_next = [0]

            def split_hi(n, w):
                unit_landed(ac, n)
                if n >= HIS:
                    ac.wait_ge(q["units_used"], n - HIS + 1)
                nc.scalar.activation(whi[:, n % HIS, 0:w], ring[:, n % RING, 0:w], ACT.Copy).then_inc(q["hi_ready"], 1)

            def expert_hi(m, job):
                expert_landed(ac, m, job)
                ac.wait_ge(q["units_used"], MOE + slot_before(m) + 1 + job * UJ)
                nc.scalar.activation(ehi[slot(m)], eraw[slot(m)], ACT.Copy).then_inc(q["hi_ready"], 1)

            def ahead(n):
                while split_next[0] <= min(n, MOE - 1):
                    split_hi(split_next[0], width(split_next[0]))
                    split_next[0] += 1

            def square_sum(r, src, dump):
                for t in range(NT):
                    if t or r:
                        ac.wait_ge(q["sq_done"], 2 * r + t)
                    nc.scalar.activation(dump, src[:, t, :], ACT.Square,
                                         accum_out=ssq[:, 2 * r + t:2 * r + t + 1]).then_inc(q["sq_done"], 1)

            def norm_hi(r, dst, nk):
                f = TR_BEFORE[r]
                for t in range(NT):
                    for k in range(0, nk, 4):
                        ac.wait_ge(q["tr_drained"], f + 1)
                        nc.scalar.activation(dst[:, k:k + 4, P * t:P * t + P], nt[:, f % 2, :].rearrange("p (k s) -> p k s", k=4),
                                             ACT.Copy).then_inc(q["t_hi"], 1)
                        f += 1

            def gemm_out(f, dst, scale=1.0, func=ACT.Copy):
                ahead(last_unit[f] + 2)
                fill_ready(ac, f)
                nc.scalar.activation(dst, PB[f % 4][:, :], func, scale=scale).then_inc(drained[f % 4], 1)

            def exp_step(s, swa):
                w = P if swa and s < 8 else S
                ac.wait_ge(q["nm_done"], s + 1)
                if s >= 2:
                    ac.wait_ge(q["t_full"], s - 1)
                    ac.wait_ge(q["p_ready"], s - 1)
                bank = PB[4 + s % 2][:, :].rearrange("p (j k) -> p j k", j=2)
                for j in range(2):
                    nc.scalar.activation(prob[:, s % 2, j, 0:w], bank[:, j, 0:w], ACT.Exp, bias=nm[:, s % 2, j:j + 1],
                                         accum_out=sm[:, s % 2, j:j + 1]).then_inc(q["exp_done"], 1)
                if swa:
                    ac.wait_ge(q["sd_done"], s + 1)
                    nc.scalar.activation(es[:, s % 2, :], sd[:, s % 2, :], ACT.Exp).then_inc(q["es_done"], 1)

            def probT_step(s, swa):
                w = 256 if swa and s < 8 else 512
                ac.wait_ge(q["t_full"], s + 1)
                if s >= 2:
                    ac.wait_ge(q["o_full"], s - 1)
                nc.scalar.activation(probT[:, s % 2, 0:w], PB[6][:, 0:w], ACT.Copy).then_inc(q["pT_ready"], 1)

            def cat_hi_step(s, tile0):
                ac.wait_ge(q["o_full"], s + 1)
                if s < 16:
                    i = nc.scalar.activation(cat_hi[:, s % 8, P * (s // 8):P * (s // 8) + P], PB[7][:, 0:P], ACT.Copy)
                else:
                    i = nc.scalar.activation(cat_hi[:, tile0:tile0 + 2, :], PB[7][:, :].rearrange("p (a b) -> p a b", a=2), ACT.Copy)
                i.then_inc(q["cat_hi_done"], 1)

            def softmax_steps(first, last, swa, tile0=0):
                exp_step(first, swa)
                for s in range(first, last):
                    if s + 1 < last:
                        exp_step(s + 1, swa)
                    if s > first:
                        cat_hi_step(s - 1, tile0 + 2 * (s - 1 - first))
                    probT_step(s, swa)
                cat_hi_step(last - 1, tile0 + 2 * (last - 1 - first))

            def memory_kv(layer):
                for j in range(4):
                    gemm_out(fills[f"k{layer}"] + j, memK[:, 2 * j:2 * j + 2, :])
                for n in range(2):
                    for t in range(NT):
                        gemm_out(fills[f"v{layer}"] + 2 * n + t, memV[:, t, 512 * n:512 * n + 512])

            def xs_copy(j):
                ac.wait_ge(q["xT_full"], j + 1)
                nc.scalar.activation(y[:, :, 256 * j:256 * j + 256], PB[6][:, :].rearrange("p (t c) -> p t c", t=NT),
                                     ACT.Copy).then_inc(q["xs_ready"], 1)

            def cross_q(layer):
                for j in range(4):
                    gemm_out(fills[f"xq{layer}"] + j, xqT[:, 2 * j:2 * j + 2, :], scale=XD ** -0.5)

            dump = actf[:, :, :].rearrange("p a b -> p (a b)")
            ac.wait_ge(q["mem_in"], 16)
            square_sum(R_MEM0, mem, dump)
            ac.wait_ge(q["x_in"], 16)
            square_sum(R_H0, x, dump)
            norm_hi(R_MEM0, memT_hi, KD)
            ahead(0)
            norm_hi(R_H0, hT_hi, KD)
            ahead(2)
            memory_kv(0)
            for j in range(4):
                gemm_out(fills["q"] + j, qT[:, 2 * j:2 * j + 2, :], scale=HD ** -0.5)
            f = fills["kv"]
            ahead(last_unit[f] + 2)
            fill_ready(ac, f)
            ac.wait_ge(q["kz_zero"], 2)
            for kv in range(2):
                for half in range(2):
                    nc.scalar.activation(kz[64 * half:64 * half + 64, kv, half, :], PB[f % 4][64 * kv:64 * kv + 64, 0:S],
                                         ACT.Copy).then_inc(q["qk_ready"], 1)
            for t in range(NT):
                i = nc.scalar.activation(vz[:, t, :, 64:128], PB[f % 4][:, 256 + 128 * t:384 + 128 * t].rearrange("p (v d) -> p v d", v=2), ACT.Copy)
                i.then_inc(drained[f % 4] if t == 1 else q["qk_ready"], 1)
            ahead(OUT0 - 1)
            softmax_steps(0, 16, True)
            cross_q(0)
            ac.wait_ge(q["mem_in"], 32)
            square_sum(R_MEM1, xn, dump)
            softmax_steps(16, 20, False, 8)
            norm_hi(R_MEM1, memT1_hi, KD)
            ahead(OUT0 + 7 + 2)
            fills_drained(ac, "out0")
            square_sum(R_F0, x, dump)
            memory_kv(1)
            norm_hi(R_F0, hT_hi, KD)
            for c in range(FC):
                ahead(FFN0 + ffn_at(c, 0) + 2)
                ac.wait_ge(q["units_used"], FFN0 + ffn_at(c, 0) + 1)
                if c >= 2:
                    ac.wait_ge(q["a_lo"], c - 1)
                nc.scalar.activation(actf[:, c % 2, :], PB[2 * (c % 2)][:, :], ACT.Silu).then_inc(q["silu_done"], 1)
                ahead(FFN0 + ffn_at(c, 1) + 2)
                ac.wait_ge(q["act_done"], c + 1)
                nc.scalar.activation(act_hi[:, c % 2], actf[:, c % 2, :].rearrange("p (k s) -> p k s", k=2), ACT.Copy).then_inc(q["a_hi"], 1)

            ahead(L1 + 2)
            ac.wait_ge(q["y_drained"], 1)
            square_sum(R_H1, x, dump)
            norm_hi(R_H1, hT_hi, KD)
            cross_q(1)
            exp_step(20, False)
            ahead(last_unit[fills["dt"]] + 2)
            nc.scalar.activation(na[:, :], pr[:, PR_ALOG:PR_ALOG + NH], ACT.Exp).then_inc(q["ln_chain"], 1)
            ac.wait_ge(q["dt_chain"], 2)
            nc.scalar.activation(dtu[:, :, :], dtr_[:, :, :], ACT.Exp, scale=-1.0).then_inc(q["ln_chain"], 1)
            ac.wait_ge(q["dt_chain"], 3)
            nc.scalar.activation(dtr_[:, :, :], dtm[:, :, :], ACT.Ln).then_inc(q["ln_chain"], 1)
            ac.wait_ge(q["u_zero"], 1)
            for j in range(12):
                f = fills["bc"] + j if j < 4 else fills["x"] + j - 4
                if j >= 2:
                    ac.wait_ge(q["conv_done"], 2 * (j - 1))
                ahead(last_unit[f] + 2)
                fill_ready(ac, f)
                nc.scalar.activation(ub[:, j % 2, :, CW - 1:], PB[f % 4][:, :].rearrange("p (a b) -> p a b", a=2), ACT.Copy).then_inc(drained[f % 4], 1)
                for k in range(2):
                    ac.wait_ge(q["conv_done"], 2 * j + k + 1)
                    if j < 4:
                        dst = BCT[:, 2 * j + k, :]
                    else:
                        if j >= 6:
                            ac.wait_ge(q["xT_full"], j - 5)
                        dst = xcT[:, j % 2, k, :]
                    nc.scalar.activation(dst, cv[:, k, :], ACT.Silu).then_inc(q["silu_conv"], 1)
                if j < 4:
                    probT_step(20 + j, False)
                    if j < 3:
                        exp_step(21 + j, False)
                    if j >= 1:
                        cat_hi_step(19 + j, 16 + 2 * (j - 1))
                if j == 4:
                    cat_hi_step(23, 22)
                if j >= 5:
                    xs_copy(j - 5)
            xs_copy(7)
            ahead(last_unit[fills["x"] + 7] + 2)
            ac.wait_ge(q["dta_full"], 1)
            nc.scalar.activation(eac[:, :], PB[4][:, 0:NH], ACT.Exp).then_inc(q["eac_done"], 1)
            nc.scalar.activation(toe[:, :], PB[4][:, 64:64 + NH], ACT.Exp).then_inc(q["eac_done"], 1)
            for s in range(2 * G):
                c, g = divmod(s, G)
                for half in range(2):
                    n = 2 * s + half
                    ac.wait_ge(q["seg_full"], n + 1)
                    if n >= 2:
                        ac.wait_ge(q["yd_full"], n // 2)
                    nc.scalar.activation(dec[:, n % 2].rearrange("p h t -> p (h t)"), PB[4 + n % 2][:, :], ACT.Exp).then_inc(q["dec_done"], 1)
                    if c == 0 and half == 0:
                        ac.wait_ge(q["bt_full"], s + 1)
                        nc.scalar.activation(btok[:, :], PB[7][:, 256:384], ACT.Copy).then_inc(q["btok_done"], 1)
                if c == 0:
                    ac.wait_ge(q["st_full"], s + 1)
                    nc.scalar.activation(st[:, g, :], PB[6][:, :], ACT.Copy).then_inc(q["st_done"], 1)
            for i in range(8):
                if i >= 2:
                    ac.wait_ge(q["yg_done"], i - 1)
                gemm_out(fills["z"] + i, zs[:, i % 2, :], func=ACT.Silu)
            ahead(last_unit[fills["z"] + 7] + 3)
            ac.wait_ge(q["yg_done"], 8)
            square_sum(R_Y, y, st[:, :, :].rearrange("p a b -> p (a b)"))
            norm_hi(R_Y, cat_hi, KI)
            ahead(last_unit[fills["out1"] + 3] + 2)
            fills_drained(ac, "out1")
            square_sum(R_F1, x, dump)
            ahead(MOE - 1)
            ac.wait_ge(q["units_used"], MOE)
            for m in range(ES - 1):
                expert_hi(m, 0)
            for t in range(NT):
                ac.wait_ge(q["hn_mul"], t + 1)
                nc.scalar.activation(hn_hi[:, t, :], xn[:, t, :], ACT.Copy).then_inc(q["hn_ready"], 1)
            ac.wait_ge(q["lg_full"], 1)
            expert_hi(ES - 1, 0)
            ac.wait_ge(q["rt_chain"], 4)
            nc.scalar.activation(pe8[:, :, :], nv1[:, :, :], ACT.Exp).then_inc(q["rt_exp"], 1)

            def gather_out(job, i):
                ac.wait_ge(q["ga_full"], 4 * job + i + 1)
                dst = (xg_hi, xg_lo)[i // 2][:, 4 * (i % 2):4 * (i % 2) + 4, :]
                nc.scalar.activation(dst, PB[GATHER_BANK[i]][:, :].rearrange("p (k s) -> p k s", k=4), ACT.Copy).then_inc(q["ga_done"], 1)

            for i in range(4):
                gather_out(0, i)
            ac.wait_ge(q["jobs_ready"], 1)
            last_job = ac.value_load(jobs_i[0:1, 0:1], min_val=NE - 1, max_val=NE - 1 + OVER)

            def expert(job, last):
                done = [ES]

                def ahead_job(m):
                    while done[0] < UJ + ES and (slot_before(done[0]) if done[0] < UJ else UJ + slot_before(done[0] - UJ)) <= m:
                        if done[0] < UJ:
                            expert_hi(done[0], job)
                        elif not last:
                            expert_hi(done[0] - UJ, job + 1)
                        done[0] += 1

                def used(m):
                    ac.wait_ge(q["units_used"], MOE + m + 1 + job * UJ)

                def silu(c):
                    w = 512 if c < FCJ - 1 else 256
                    m = job_unit(c, 0) + (1 if c < FCJ - 1 else 0)
                    ahead_job(m - 1)
                    used(m)
                    nc.scalar.activation(actf[:, c % 2, 0:w], PB[2 * (c % 2)][:, 0:w], ACT.Silu).then_inc(q["e_silu"], 1)

                def turn_hi(c):
                    nk = 4 if c < FCJ - 1 else 2
                    ac.wait_ge(q["e_t"], FCJ * job + c + 1)
                    nc.scalar.activation(aT_hi[:, c % 2, 0:nk, :], PB[4][:, 0:P * nk].rearrange("p (k s) -> p k s", k=nk), ACT.Copy).then_inc(q["e_thi"], 1)

                silu(0)
                silu(1)
                turn_hi(0)
                for c in range(2, FCJ - 1):
                    silu(c)
                    turn_hi(c - 1)
                    if c == 2:
                        ahead_job(job_unit(1, 2))
                        ac.wait_ge(q["selT_full"], job + 1)
                        nc.scalar.activation(selT, PB[7][:, 0:S].rearrange("p (t s) -> p t s", t=NT), ACT.Copy).then_inc(q["selT_done"], 1)
                silu(FCJ - 1)
                turn_hi(FCJ - 2)
                ahead_job(29)
                if not last:
                    gather_out(job + 1, 0)
                    gather_out(job + 1, 1)
                ahead_job(30)
                turn_hi(FCJ - 1)
                if not last:
                    gather_out(job + 1, 2)
                    ahead_job(31)
                    gather_out(job + 1, 3)
                ahead_job(31)
                used(UJ - 1)
                for n in range(2):
                    nc.scalar.activation(y_hi[:, 512 * n:512 * n + 512], PB[5 + n][:, :], ACT.Copy).then_inc(q["yhi_done"], 1)
                ahead_job(32)

            with ac.Fori(0, last_job) as job:
                expert(job, False)
            expert(last_job, True)
            ac.wait_ge(q["sc_done"], 4 * last_job + 8)
            square_sum(R_FIN, x, dump)

        @block.vector
        def _(ve):
            split_next = [0]

            def split_lo(n, w):
                ve.wait_ge(q["hi_ready"], n + 1)
                if n >= LOS:
                    ve.wait_ge(q["units_used"], n - LOS + 1)
                ve.tensor_tensor(wlo[:, n % LOS, 0:w], ring[:, n % RING, 0:w], whi[:, n % HIS, 0:w].bitcast(F32),
                                 ALU.subtract).then_inc(q["lo_ready"], 1)

            def expert_lo(m, job):
                ve.wait_ge(q["hi_ready"], MOE + m + 1 + job * UJ)
                ve.tensor_tensor(elo[slot(m)], eraw[slot(m)], ehi[slot(m)].bitcast(F32), ALU.subtract).then_inc(q["lo_ready"], 1)

            def ahead(n):
                while split_next[0] <= min(n, MOE - 1):
                    split_lo(split_next[0], width(split_next[0]))
                    split_next[0] += 1

            def norm_T(r, src, g0, dst, width, into):
                nk = width // P
                for t in range(NT):
                    c = 2 * r + t
                    ve.wait_ge(q["rstd_done"], c + 1)
                    ve.tensor_scalar(into[:, t, :], src[:, t, :], rstd[:, c:c + 1], None, ALU.mult).then_inc(q["xn_done"], 1)
                f0 = TR_BEFORE[r]
                order = [(t, k) for t in range(NT) for k in range(0, nk, 4)]

                def lo(i):
                    t, k = order[i]
                    ve.wait_ge(q["t_hi"], f0 + i + 1)
                    d = (slice(None), slice(k, k + 4), slice(P * t, P * t + P))
                    ve.tensor_tensor(dst[1][d], nt[:, (f0 + i) % 2, :].rearrange("p (k s) -> p k s", k=4), dst[0][d].bitcast(F32),
                                     ALU.subtract).then_inc(q["t_lo"], 1)

                for i, (t, k) in enumerate(order):
                    f = f0 + i
                    ve.wait_ge(q["tr_full"], f + 1)
                    if f >= 2 and dst is not None:
                        ve.wait_ge(q["t_lo"], f - 1)
                    prod = hTf[:, k:k + 4, P * t:P * t + P] if dst is None else nt[:, f % 2, :].rearrange("p (k s) -> p k s", k=4)
                    ve.tensor_tensor(prod, PB[4 + f % 2][:, :].rearrange("p (k s) -> p k s", k=4),
                                     pc[:, g0 + k:g0 + k + 4].unsqueeze(2).to_broadcast([P, 4, P]), ALU.mult).then_inc(q["tr_drained"], 1)
                    if i and dst is not None:
                        lo(i - 1)
                if dst is not None:
                    lo(len(order) - 1)

            def max_step(s, swa):
                w = P if swa and s < 8 else S
                ve.wait_ge(q["s_full"], s + 1)
                bank = PB[4 + s % 2][:, :].rearrange("p (j k) -> p j k", j=2)[:, :, 0:w]
                if s >= 2:
                    ve.wait_ge(q["exp_done"], 2 * (s - 1))
                if swa:
                    ve.tensor_reduce(mx[:, s % 2, :], bank, AX_X, ALU.max).then_inc(q["mx_done"], 1)
                    ve.wait_ge(q["mx_done"], s + 1)
                    ve.scalar_tensor_tensor(out=nm[:, s % 2, :], in0=mx[:, s % 2, :], scalar=-1.0,
                                            in1=nsink[:, 2 * (s % 8):2 * (s % 8) + 2], op0=ALU.mult, op1=ALU.min).then_inc(q["nm_done"], 1)
                    ve.wait_ge(q["nm_done"], s + 1)
                    if s >= 2:
                        ve.wait_ge(q["es_done"], s - 1)
                    ve.tensor_tensor(sd[:, s % 2, :], nm[:, s % 2, :], nsink[:, 2 * (s % 8):2 * (s % 8) + 2], ALU.subtract).then_inc(q["sd_done"], 1)
                else:
                    ve.tensor_reduce(nm[:, s % 2, :], bank, AX_X, ALU.max, negate=True).then_inc(q["nm_done"], 1)

            def norm_step(s, swa):
                w = P if swa and s < 8 else S
                ve.wait_ge(q["exp_done"], 2 * s + 2)
                if swa:
                    ve.wait_ge(q["es_done"], s + 1)
                    ve.tensor_tensor(den[:, s % 2, :], sm[:, s % 2, :], es[:, s % 2, :], ALU.add).then_inc(q["den_done"], 1)
                    ve.wait_ge(q["den_done"], s + 1)
                    ve.reciprocal(rden[:, s % 2, :], den[:, s % 2, :]).then_inc(q["rden_done"], 1)
                else:
                    ve.reciprocal(rden[:, s % 2, :], sm[:, s % 2, :]).then_inc(q["rden_done"], 1)
                ve.wait_ge(q["rden_done"], s + 1)
                pv = prob[:, s % 2, :, 0:w]
                ve.tensor_tensor(pv, pv, rden[:, s % 2, :].unsqueeze(2).to_broadcast([P, 2, w]), ALU.mult).then_inc(q["p_ready"], 1)

            def cat_step(s, tile0):
                ve.wait_ge(q["cat_hi_done"], s + 1)
                if s < 16:
                    d = (slice(None), s % 8, slice(P * (s // 8), P * (s // 8) + P))
                    src = PB[7][:, 0:P]
                else:
                    d = (slice(None), slice(tile0, tile0 + 2), slice(None))
                    src = PB[7][:, :].rearrange("p (a b) -> p a b", a=2)
                ve.tensor_tensor(cat_lo[d], src, cat_hi[d].bitcast(F32), ALU.subtract).then_inc(q["cat_done"], 1)

            def softmax_steps(first, last, swa, tile0=0):
                max_step(first, swa)
                for s in range(first, last):
                    if s + 1 < last:
                        max_step(s + 1, swa)
                    norm_step(s, swa)
                    if s > first:
                        cat_step(s - 1, tile0 + 2 * (s - 1 - first))
                cat_step(last - 1, tile0 + 2 * (last - 1 - first))

            def add_out(name):
                for n in range(2):
                    for t in range(NT):
                        f = fills[name] + 2 * n + t
                        ahead(last_unit[f] + 2)
                        fill_ready(ve, f)
                        xv = x[:, t, 512 * n:512 * n + 512]
                        ve.tensor_tensor(xv, xv, PB[f % 4][:, :], ALU.add).then_inc(drained[f % 4], 1)
                fills_drained(ve, name)

            ve.wait_ge(q["par_in"], 48)
            ve.tensor_scalar(nsink[:, :], pr[:, PR_SINK:PR_SINK + HQ], -1.0, None, ALU.mult).then_inc(q["nsink_set"], 1)
            ve.memset(brow[:, :], NEG).then_inc(q["brow_set"], 1)
            ve.wait_ge(q["mem_in"], 16)
            norm_T(R_MEM0, mem, PC_MEM, (memT_hi, memT_lo), D, xn)
            ve.wait_ge(q["bias_full"], 1)
            ve.wait_ge(q["brow_set"], 1)
            ve.tensor_copy(brow[:, P:2 * P], PB[6][0:HQ, 0:P]).then_inc(q["brow_done"], 1)
            ahead(0)
            ve.wait_ge(q["x_in"], 16)
            ve.wait_ge(q["tr_full"], 4)
            norm_T(R_H0, x, PC_MIX, (hT_hi, hT_lo), D, xn)
            ve.wait_ge(q["nsink_set"], 1)
            ahead(OUT0 - 1)
            softmax_steps(0, 16, True)
            ve.wait_ge(q["mem_in"], 32)
            softmax_steps(16, 20, False, 8)
            norm_T(R_MEM1, xn, PC_MEM + 8, (memT1_hi, memT1_lo), D, xn)
            add_out("out0")
            ve.wait_ge(q["tr_full"], 12)
            ahead(KV1 + 2)
            ahead(last_unit[fills["v1"] + 3] + 1)
            norm_T(R_F0, x, PC_FFN, (hT_hi, hT_lo), D, xn)
            ahead(FFN0 + 1)
            for c in range(FC):
                ahead(FFN0 + ffn_at(c, 1) + 2)
                ve.wait_ge(q["units_used"], FFN0 + ffn_at(c, 1) + 1)
                ve.wait_ge(q["silu_done"], c + 1)
                ve.tensor_tensor(actf[:, c % 2, :], actf[:, c % 2, :], PB[2 * (c % 2) + 1][:, :], ALU.mult).then_inc(q["act_done"], 1)
                ve.wait_ge(q["a_hi"], c + 1)
                ve.tensor_tensor(act_lo[:, c % 2], actf[:, c % 2, :].rearrange("p (k s) -> p k s", k=2), act_hi[:, c % 2].bitcast(F32),
                                 ALU.subtract).then_inc(q["a_lo"], 1)
            ahead(L1 + 1)
            ve.wait_ge(q["units_used"], FFN0 + 3 * FC)
            for t in range(NT):
                for n in range(2):
                    xv = x[:, t, 512 * n:512 * n + 512]
                    i = ve.tensor_tensor(xv, xv, PB[4 + 2 * n + t][:, :], ALU.add)
            i.then_inc(q["y_drained"], 1)
            ve.wait_ge(q["y_drained"], 1)
            norm_T(R_H1, x, PC_MIX + 8, (hT_hi, hT_lo), D, xn)
            ahead(last_unit[fills["xq1"] + 3] + 1)
            max_step(20, False)
            norm_step(20, False)

            f = fills["dt"]
            ahead(last_unit[f] + 1)
            fill_ready(ve, f)
            ve.tensor_tensor(dtx[:, :, :], PB[f % 4][:, 0:64].rearrange("p (t h) -> p t h", t=NT),
                             pr[:, PR_DTB:PR_DTB + NH].unsqueeze(1).to_broadcast([P, NT, NH]), ALU.add).then_inc(drained[f % 4], 1)
            ve.wait_ge(drained[f % 4], f // 4 + 1)
            chain = 0

            def link(i):
                nonlocal chain
                chain += 1
                i.then_inc(q["dt_chain"], 1)
                ve.wait_ge(q["dt_chain"], chain)

            link(ve.tensor_scalar(dtm[:, :, :], dtx[:, :, :], -1.0, None, ALU.mult))
            link(ve.tensor_tensor(dtr_[:, :, :], dtm[:, :, :], dtx[:, :, :], ALU.max))
            ahead(last_unit[f] + 2)
            ve.wait_ge(q["ln_chain"], 2)
            link(ve.tensor_scalar(dtm[:, :, :], dtu[:, :, :], 1.0, None, ALU.add))
            ve.wait_ge(q["ln_chain"], 3)
            link(ve.tensor_scalar(dtm[:, :, :], dtm[:, :, :], -1.0, None, ALU.add))
            link(ve.tensor_scalar(dt[:, :, :], dtm[:, :, :], 0.0, None, ALU.is_equal))
            link(ve.tensor_tensor(dtm[:, :, :], dtm[:, :, :], dt[:, :, :], ALU.add))
            link(ve.tensor_tensor(dtr_[:, :, :], dtr_[:, :, :], dt[:, :, :], ALU.add))
            link(ve.reciprocal(dtm[:, :, :], dtm[:, :, :]))
            link(ve.tensor_tensor(dtr_[:, :, :], dtr_[:, :, :], dtu[:, :, :], ALU.mult))
            link(ve.tensor_tensor(dtr_[:, :, :], dtr_[:, :, :], dtm[:, :, :], ALU.mult))
            link(ve.scalar_tensor_tensor(out=dt[:, :, :], in0=dtx[:, :, :], scalar=0.0, in1=dtr_[:, :, :], op0=ALU.max, op1=ALU.add))
            link(ve.scalar_tensor_tensor(out=dta[:, :, :], in0=dt[:, :, :], scalar=-1.0,
                                         in1=na[:, :].unsqueeze(1).to_broadcast([P, NT, NH]), op0=ALU.mult, op1=ALU.mult))
            ve.memset(ub[:, :, :, 0:CW - 1], 0.0).then_inc(q["u_zero"], 1)
            ve.wait_ge(q["u_zero"], 1)
            ve.memset(stat[:, 0:1], 0.0).then_inc(q["dt_ready"], 1)
            cc = 0
            for j in range(12):
                f = fills["bc"] + j if j < 4 else fills["x"] + j - 4
                ahead(last_unit[f] + 2)
                ve.wait_ge(drained[f % 4], f // 4 + 1)
                for k in range(2):
                    tile = 16 + 2 * j + k if j < 4 else 2 * (j - 4) + k
                    n = 2 * j + k
                    if n >= 2:
                        ve.wait_ge(q["silu_conv"], n - 1)
                    u = ub[:, j % 2, k, :]
                    w = pc[:, PC_CW + CW * tile:PC_CW + CW * tile + CW]
                    ve.tensor_scalar(cv[:, k, :], u[:, CW - 1:], w[:, CW - 1:CW], pc[:, PC_CB + tile:PC_CB + tile + 1], ALU.mult, ALU.add).then_inc(q["conv_chain"], 1)
                    cc += 1
                    for tap in range(CW - 2, -1, -1):
                        ve.wait_ge(q["conv_chain"], cc)
                        i = ve.scalar_tensor_tensor(out=cv[:, k, :], in0=u[:, tap:tap + S], scalar=w[:, tap:tap + 1], in1=cv[:, k, :],
                                                    op0=ALU.mult, op1=ALU.add)
                        if tap:
                            cc += 1
                            i.then_inc(q["conv_chain"], 1)
                        else:
                            i.then_inc(q["conv_done"], 1)
                if j < 3:
                    max_step(21 + j, False)
                    norm_step(21 + j, False)
                if 1 <= j <= 4:
                    cat_step(19 + j, 16 + 2 * (j - 1))
            for s in range(2 * G):
                c, g = divmod(s, G)
                ve.wait_ge(q["cb_full"], s + 1)
                if s >= 1:
                    ve.wait_ge(q["m_ready"], 2 * s)
                ve.tensor_tensor(cbm[:, :], PB[7][:, 0:P], tri, ALU.mult).then_inc(q["cbm_done"], 1)
                ve.wait_ge(q["cbm_done"], s + 1)
                for half in range(2):
                    n = 2 * s + half
                    ve.wait_ge(q["dec_done"], n + 1)
                    dv = dec[:, n % 2]
                    ve.tensor_tensor(dv, dv, cbm[:, :].unsqueeze(1).to_broadcast([P, 4, P]), ALU.mult).then_inc(q["m_ready"], 1)
                xs = y[:, c, 512 * g:512 * g + 512]
                ve.wait_ge(q["xsD_ready"], s + 1)
                ve.wait_ge(q["yd_full"], s + 1)
                i = ve.tensor_tensor(xs, xsD[:, :, :].rearrange("p h d -> p (h d)"), PB[2 + s % 2][:, :], ALU.add)
                if c == 0:
                    i.then_inc(q["yy_done"], 1)
                else:
                    i.then_inc(q["yo_done"], 1)
                    ve.wait_ge(q["yo_full"], s - G + 1)
                    ve.tensor_tensor(yo[:, :].rearrange("p (h d) -> p h d", h=HPG), PB[6][:, :].rearrange("p (h d) -> p h d", h=HPG),
                                     eac[:, HPG * g:HPG * g + HPG].unsqueeze(2).to_broadcast([P, HPG, PH]), ALU.mult).then_inc(q["yo_done"], 1)
                    ve.wait_ge(q["yo_done"], 2 * (s - G + 1))
                    ve.tensor_tensor(xs, xs, yo[:, :], ALU.add).then_inc(q["yy_done"], 1)
            ve.wait_ge(q["yy_done"], 2 * G)
            for n in range(4):
                for t in range(NT):
                    i = 2 * n + t
                    f = fills["z"] + i
                    ahead(last_unit[f] + 2)
                    ve.wait_ge(drained[f % 4], f // 4 + 1)
                    yv = y[:, t, 512 * n:512 * n + 512]
                    ve.tensor_tensor(yv, yv, zs[:, i % 2, :], ALU.mult).then_inc(q["yg_done"], 1)
            norm_T(R_Y, y, PC_GN, (cat_hi, cat_lo), DI, y)
            add_out("out1")
            ahead(MOE - 1)
            ve.wait_ge(q["units_used"], MOE)
            expert_lo(0, 0)
            norm_T(R_F1, x, PC_FFN + 8, None, D, xn)

            chain = 0

            def rlink(i):
                nonlocal chain
                chain += 1
                i.then_inc(q["rt_chain"], 1)
                ve.wait_ge(q["rt_chain"], chain)

            ve.wait_ge(q["lg_full"], 1)
            rlink(ve.tensor_copy(lg[:, :, :], PB[0][:, 0:16].rearrange("p (t e) -> p t e", t=NT)))
            rlink(ve.tensor_reduce(s8[:, :], lg[:, :, :], AX_X, ALU.max))
            for t in range(NT):
                rlink(ve.tensor_scalar(nv1[:, t, :], lg[:, t, :], s8[:, t:t + 1], None, ALU.subtract))
            for t in range(NT):
                mine = lg[:, t, :].unsqueeze(2).to_broadcast([P, NE, NE])
                other = lg[:, t, :].unsqueeze(1).to_broadcast([P, NE, NE])
                rlink(ve.tensor_tensor(cmp1[:, t], other, mine, ALU.is_gt))
                rlink(ve.tensor_tensor(cmp2[:, t], other, mine, ALU.is_equal))
                rlink(ve.tensor_tensor(cmp2[:, t], cmp2[:, t], con[:, C_LT:C_LT + 64].rearrange("p (e j) -> p e j", e=NE), ALU.mult))
                rlink(ve.tensor_tensor(cmp1[:, t], cmp1[:, t], cmp2[:, t], ALU.add))
                rlink(ve.tensor_reduce(rank[:, t, :], cmp1[:, t], AX_X, ALU.add))
            ve.tensor_scalar(top[:, :, :], rank[:, :, :], 2.0, None, ALU.is_lt).then_inc(q["top_done"], 1)
            ve.wait_ge(q["top_done"], 1)
            ve.wait_ge(q["late_in"], 32)
            for t in range(NT):
                ve.tensor_tensor(xn[:, t, :], xn[:, t, :], grow[:, :], ALU.mult).then_inc(q["hn_mul"], 1)
            ve.wait_ge(q["rt_exp"], 1)
            rlink(ve.tensor_tensor(pe8[:, :, :], pe8[:, :, :], top[:, :, :], ALU.mult))
            rlink(ve.tensor_reduce(s8[:, :], pe8[:, :, :], AX_X, ALU.add))
            rlink(ve.reciprocal(s8[:, :], s8[:, :]))
            rlink(ve.tensor_tensor(comb[:, :, :], pe8[:, :, :], s8[:, :].unsqueeze(2).to_broadcast([P, NT, NE]), ALU.mult))
            rlink(ve.memset(jobcomb[:, :, 0:1], 0.0))
            rlink(ve.tensor_copy(jobcomb[:, :, 1:1 + NE], comb[:, :, :]))
            ve.wait_ge(q["pos_full"], 1)
            rlink(ve.scalar_tensor_tensor(out=posm[:, :, :], in0=PB[1][:, 0:16].rearrange("p (t e) -> p t e", t=NT), scalar=1.0, in1=top[:, :, :],
                                          op0=ALU.add, op1=ALU.mult))
            rlink(ve.tensor_scalar(posm[:, :, :], posm[:, :, :], -1.0, None, ALU.add))
            rlink(ve.tensor_copy(jobpos[:, :, 0:NE], posm[:, :, :]))
            rlink(ve.tensor_scalar(full[:, :], PB[1][:, 16:24], float(SLOTS), None, ALU.is_gt))

            def choose(job):
                for t in range(NT):
                    i = ve.tensor_scalar(sel[:, t, :], con[:, C_IO:C_IO + P], jobpos[:, t, bass.ds(job, 1)], None, ALU.is_equal)
                i.then_inc(q["sel_ready"], 1)

            choose(0)
            for t in range(NT):
                ve.wait_ge(q["hn_ready"], t + 1)
                i = ve.tensor_tensor(hn_lo[:, t, :], xn[:, t, :], hn_hi[:, t, :].bitcast(F32), ALU.subtract)
            i.then_inc(q["hn_ready"], 1)
            ve.wait_ge(q["hn_ready"], 3)
            before_of = cmp1[:, 0]
            rlink(ve.tensor_tensor(before_of, full[:, :].unsqueeze(1).to_broadcast([P, NE, NE]),
                                   con[:, C_LT:C_LT + 64].rearrange("p (e j) -> p e j", e=NE), ALU.mult))
            rlink(ve.tensor_reduce(before[:, :], before_of, AX_X, ALU.add))
            rlink(ve.tensor_tensor(oh[:, :, :], before[:, :].unsqueeze(1).to_broadcast([P, OVER, NE]),
                                   con[:, C_K:C_K + OVER * NE].rearrange("p (k e) -> p k e", k=OVER), ALU.is_equal))
            rlink(ve.tensor_tensor(oh[:, :, :], oh[:, :, :], full[:, :].unsqueeze(1).to_broadcast([P, OVER, NE]), ALU.mult))
            rlink(ve.tensor_tensor(pick[:, :, :], oh[:, :, :], con[:, C_E:C_E + NE].unsqueeze(1).to_broadcast([P, OVER, NE]), ALU.mult))
            rlink(ve.tensor_reduce(overe[:, :], pick[:, :, :], AX_X, ALU.add))
            rlink(ve.tensor_copy(overe_i[:, :], overe[:, :]))
            for t in range(NT):
                rlink(ve.tensor_tensor(pick[:, :, :], oh[:, :, :], posm[:, t, :].unsqueeze(1).to_broadcast([P, OVER, NE]), ALU.mult))
                rlink(ve.tensor_reduce(jobpos[:, t, NE:], pick[:, :, :], AX_X, ALU.add))
                rlink(ve.tensor_scalar(jobpos[:, t, NE:], jobpos[:, t, NE:], float(-SLOTS), None, ALU.add))
                rlink(ve.tensor_tensor(pick[:, :, :], oh[:, :, :], comb[:, t, :].unsqueeze(1).to_broadcast([P, OVER, NE]), ALU.mult))
                rlink(ve.tensor_reduce(jobcomb[:, t, 1 + NE:], pick[:, :, :], AX_X, ALU.add))
            rlink(ve.tensor_reduce(jobs[:, :], full[:, :], AX_X, ALU.add))
            rlink(ve.tensor_scalar(jobs[:, :], jobs[:, :], float(NE - 1), None, ALU.add))
            ve.tensor_copy(jobs_i[:, :], jobs[:, :]).then_inc(q["jobs_ready"], 1)
            ve.wait_ge(q["jobs_ready"], 1)
            for m in range(1, ES):
                expert_lo(m, 0)
            ve.memset(y_hi.bitcast(F32), 0.0)
            ve.memset(selT.bitcast(F32), 0.0).then_inc(q["selT_done"], 1)
            ve.memset(y_lo.bitcast(F32), 0.0).then_inc(q["ylo_done"], 2)
            last_job = ve.value_load(jobs_i[0:1, 0:1], min_val=NE - 1, max_val=NE - 1 + OVER)

            def scatter_add(job, i):
                t, n = divmod(i, 2)
                ve.wait_ge(q["sc_full"], 4 * job + i + 1)
                xv = x[:, t, 512 * n:512 * n + 512]
                ve.scalar_tensor_tensor(out=xv, in0=PB[7][:, :], scalar=jobcomb[:, t, bass.ds(job, 1)], in1=xv,
                                        op0=ALU.mult, op1=ALU.add).then_inc(q["sc_done"], 1)

            def expert(job, last):
                done = [ES]

                def ahead_job(m):
                    while done[0] < UJ + ES and (slot_before(done[0]) if done[0] < UJ else UJ + slot_before(done[0] - UJ)) <= m:
                        if done[0] < UJ:
                            expert_lo(done[0], job)
                        elif not last:
                            expert_lo(done[0] - UJ, job + 1)
                        done[0] += 1

                def times_up(c):
                    w = 512 if c < FCJ - 1 else 256
                    m = job_unit(c, 1) + (1 if c < FCJ - 1 else 0)
                    ahead_job(m - 1)
                    ve.wait_ge(q["units_used"], MOE + m + 1 + job * UJ)
                    ve.wait_ge(q["e_silu"], FCJ * job + c + 1)
                    ve.tensor_tensor(actf[:, c % 2, 0:w], actf[:, c % 2, 0:w], PB[2 * (c % 2) + 1][:, 0:w], ALU.mult).then_inc(q["e_act"], 1)

                def turn_lo(c):
                    nk = 4 if c < FCJ - 1 else 2
                    ve.wait_ge(q["e_thi"], FCJ * job + c + 1)
                    ve.tensor_tensor(aT_lo[:, c % 2, 0:nk, :], PB[4][:, 0:P * nk].rearrange("p (k s) -> p k s", k=nk),
                                     aT_hi[:, c % 2, 0:nk, :].bitcast(F32), ALU.subtract).then_inc(q["e_tlo"], 1)

                times_up(0)
                ahead_job(4)
                scatter_add(job, 0)
                turn_lo(0)
                ahead_job(5)
                scatter_add(job, 1)
                times_up(1)
                ahead_job(job_unit(0, 2))
                scatter_add(job, 2)
                for c in range(2, FCJ - 1):
                    ahead_job(job_unit(c, 0))
                    if c == 2:
                        scatter_add(job, 3)
                    turn_lo(c - 1)
                    if c == 3 and not last:
                        choose(job + 1)
                    times_up(c)
                ahead_job(28)
                turn_lo(FCJ - 2)
                times_up(FCJ - 1)
                ahead_job(30)
                turn_lo(FCJ - 1)
                ahead_job(31)
                for n in range(2):
                    ve.wait_ge(q["yhi_done"], 2 * job + n + 1)
                    ve.tensor_tensor(y_lo[:, 512 * n:512 * n + 512], PB[5 + n][:, :], y_hi[:, 512 * n:512 * n + 512].bitcast(F32),
                                     ALU.subtract).then_inc(q["ylo_done"], 1)
                ahead_job(32)

            with ve.Fori(0, last_job) as job:
                expert(job, False)
            expert(last_job, True)
            for i in range(4):
                scatter_add(last_job + 1, i)
            for t in range(NT):
                c = 2 * R_FIN + t
                ve.wait_ge(q["rstd_done"], c + 1)
                ve.scalar_tensor_tensor(out=xn[:, t, :], in0=x[:, t, :], scalar=rstd[:, c:c + 1], in1=gfin[:, :],
                                        op0=ALU.mult, op1=ALU.mult).then_inc(q["final"], 1)

        @block.tensor
        def _(pe):
            mm = nc.tensor.matmul

            def mm3(out, lhs, rhs, start, stop):
                mm(out, lhs[0], rhs[0], start=start, stop=False)
                mm(out, lhs[0], rhs[1], start=False, stop=False)
                return mm(out, lhs[1], rhs[0], start=False, stop=stop)

            def cut(pair, *index):
                return pair[0][index], pair[1][index]

            ALL = slice(None)
            hT, memT, memT1, cat, act = (hT_hi, hT_lo), (memT_hi, memT_lo), (memT1_hi, memT1_lo), (cat_hi, cat_lo), (act_hi, act_lo)

            def transposed(r, src, width):
                f = TR_BEFORE[r]
                for t in range(NT):
                    pe.wait_ge(q["xn_done"], 2 * r + t + 1)
                    for k in range(0, width // P, 4):
                        if f >= 2:
                            pe.wait_ge(q["tr_drained"], f - 1)
                        for i in range(4):
                            last = nc.tensor.transpose(PB[4 + f % 2][:, P * i:P * i + P], src[:, t, P * (k + i):P * (k + i) + P], ident)
                        last.then_inc(q["tr_full"], 1)
                        f += 1

            def bank_free(f):
                if f >= 4:
                    pe.wait_ge(drained[f % 4], f // 4)

            def split_ready(n, job=0):
                pe.wait_ge(q["lo_ready"], n + 1 + job * UJ)

            def gemm_a(n, bank, actT):
                w = parts(n, "a")
                for c in range(2):
                    for k in range(KD):
                        last = mm3(bank[:, S * c:S * c + S], cut(w, ALL, k, slice(P * c, P * c + P)), cut(actT, ALL, k), k == 0, k == KD - 1)
                last.then_inc(q["units_used"], 1)

            def gemm_a_fill(n, f, actT):
                split_ready(n)
                bank_free(f)
                gemm_a(n, PB[f % 4], actT)

            def gemm_b(n, f, kgs, actT):
                for kg in range(kgs):
                    split_ready(n + kg)
                    w = parts(n + kg, "b")
                    for t in range(NT):
                        if kg == 0:
                            bank_free(f + t)
                        for k in range(4):
                            kk = 4 * kg + k
                            last = mm3(PB[(f + t) % 4][:, :], cut(actT, ALL, kk, slice(P * t, P * t + P)), cut(w, ALL, k), kk == 0, kk == 4 * kgs - 1)
                    last.then_inc(q["units_used"], 1)

            def memory_kv(layer, n, m):
                for j in range(4):
                    gemm_a_fill(n + j, fills[f"k{layer}"] + j, m)
                for j in range(2):
                    gemm_b(n + 4 + 2 * j, fills[f"v{layer}"] + 2 * j, 2, m)

            def scores(s, swa):
                if s >= 2:
                    pe.wait_ge(q["exp_done"], 2 * (s - 1))
                bank = PB[4 + s % 2]
                if swa:
                    b, hp = divmod(s, 8)
                    w = P if b == 0 else S
                    kv = hp // 4
                    for j in range(2):
                        o = bank[:, S * j:S * j + w]
                        h = 2 * hp + j
                        mm(o, antiJ, hankel[h // 8][:, h % 8, S - w:S].bitcast(F32), start=True, stop=False)
                        last = mm(o, qT[:, hp, P * b:P * b + P], kz[:, kv, j, P * b + P - w:P * b + P], start=False, stop=True)
                else:
                    h = s % 4
                    for j in range(NT):
                        for k in range(2):
                            last = mm(bank[:, S * j:S * j + S], xqT[:, 2 * h + k, P * j:P * j + P], memK[:, 2 * h + k, :], start=k == 0, stop=k == 1)
                last.then_inc(q["s_full"], 1)

            def transpose_probs(s, swa):
                nk = 1 if swa and s < 8 else 2
                pe.wait_ge(q["p_ready"], s + 1)
                if s >= 1:
                    pe.wait_ge(q["pT_ready"], s)
                for k in range(nk):
                    for j in range(2):
                        last = nc.tensor.transpose(PB[6][:, P * (2 * k + j):P * (2 * k + j) + P], prob[:, s % 2, j, P * k:P * k + P], ident)
                last.then_inc(q["t_full"], 1)

            def values(s, swa):
                pe.wait_ge(q["pT_ready"], s + 1)
                if s >= 1:
                    pe.wait_ge(q["cat_done"], s)
                pt = probT[:, s % 2, :]
                if swa:
                    b, hp = divmod(s, 8)
                    nk = 1 if b == 0 else 2
                    kv = hp // 4
                    for k in range(nk):
                        t = b - nk + 1 + k
                        for j in range(2):
                            last = mm(PB[7][:, 0:P], vz[:, t, kv, 64 - 64 * j:192 - 64 * j], pt[:, P * (2 * k + j):P * (2 * k + j) + P],
                                      start=k == 0 and j == 0, stop=k == nk - 1 and j == 1)
                else:
                    h = s % 4
                    for d in range(2):
                        for k in range(2):
                            last = mm(PB[7][:, S * d:S * d + S], memV[:, k, XD * h + P * d:XD * h + P * d + P], pt[:, S * k:S * k + S],
                                      start=k == 0, stop=k == 1)
                last.then_inc(q["o_full"], 1)

            def softmax_steps(first, last, swa):
                scores(first, swa)
                for s in range(first, last):
                    if s + 1 < last:
                        scores(s + 1, swa)
                    if s > first:
                        values(s - 1, swa)
                    transpose_probs(s, swa)
                values(last - 1, swa)

            pe.wait_ge(q["par_in"], 48)
            transposed(R_MEM0, xn, D)
            pe.wait_ge(q["rel_in"], 32)
            mm(PB[6][0:HQ, 0:P], rel[:, :], buck[:, :], start=True, stop=True).then_inc(q["bias_full"], 1)
            transposed(R_H0, xn, D)
            pe.wait_ge(q["t_lo"], 4)
            memory_kv(0, 0, memT)
            pe.wait_ge(q["t_lo"], 8)
            for j in range(4):
                gemm_a_fill(8 + j, fills["q"] + j, hT)
            n, f = 12, fills["kv"]
            split_ready(n)
            bank_free(f)
            w = parts(n, "a")
            for k in range(KD):
                mm3(PB[f % 4][:, 0:S], cut(w, ALL, k, slice(0, P)), cut(hT, ALL, k), k == 0, k == KD - 1)
            for t in range(NT):
                for k in range(KD):
                    last = mm3(PB[f % 4][:, S + P * t:S + P * t + P], cut(hT, ALL, k, slice(P * t, P * t + P)), cut(w, ALL, k, slice(P, 2 * P)),
                               k == 0, k == KD - 1)
            last.then_inc(q["units_used"], 1)
            for j in range(4):
                gemm_a_fill(13 + j, fills["xq0"] + j, hT)
            pe.wait_ge(q["hank_in"], 32)
            pe.wait_ge(drained[fills["kv"] % 4], fills["kv"] // 4 + 1)
            pe.wait_ge(q["qk_ready"], 5)
            softmax_steps(0, 16, True)
            fills_drained(pe, "xq0")
            softmax_steps(16, 20, False)
            pe.wait_ge(q["cat_done"], 20)
            transposed(R_MEM1, xn, D)
            for j in range(2):
                gemm_b(OUT0 + 4 * j, fills["out0"] + 2 * j, 4, cat)
            pe.wait_ge(q["t_lo"], 12)
            memory_kv(1, KV1, memT1)
            transposed(R_F0, xn, D)
            pe.wait_ge(q["t_lo"], 16)

            def down(c):
                n = FFN0 + ffn_at(c, 2)
                split_ready(n)
                pe.wait_ge(q["a_lo"], c + 1)
                w = parts(n, "d")
                for t in range(NT):
                    for nn in range(2):
                        for k in range(2):
                            last = mm3(PB[4 + 2 * nn + t][:, :], cut(act, ALL, c % 2, k, slice(P * t, P * t + P)),
                                       cut(w, ALL, k, slice(512 * nn, 512 * nn + 512)), c == 0 and k == 0, c == FC - 1 and k == 1)
                last.then_inc(q["units_used"], 1)

            fills_drained(pe, "v1")
            for c in range(FC):
                for part in range(2):
                    n = FFN0 + ffn_at(c, part)
                    split_ready(n)
                    if c >= 2:
                        pe.wait_ge(q["act_done"], c - 1)
                    gemm_a(n, PB[2 * (c % 2) + part], hT)
                if c:
                    down(c - 1)
            down(FC - 1)

            pe.wait_ge(q["y_drained"], 1)
            transposed(R_H1, xn, D)
            pe.wait_ge(q["t_lo"], 20)
            for j in range(4):
                gemm_a_fill(L1 + j, fills["xq1"] + j, hT)
            fills_drained(pe, "xq1")
            scores(20, False)
            n, f = L1 + 4, fills["dt"]
            split_ready(n)
            bank_free(f)
            w = parts(n, "t")
            for t in range(NT):
                for k in range(KD):
                    last = mm3(PB[f % 4][:, NH * t:NH * t + NH], cut(hT, ALL, k, slice(P * t, P * t + P)), cut(w, ALL, k), k == 0, k == KD - 1)
            last.then_inc(q["units_used"], 1)
            for j in range(4):
                gemm_a_fill(L1 + 5 + j, fills["bc"] + j, hT)
                transpose_probs(20 + j, False)
                if j < 3:
                    scores(21 + j, False)
                if j >= 1:
                    values(19 + j, False)

            def x_transposes(j):
                pe.wait_ge(q["silu_conv"], 2 * j + 10)
                if j >= 1:
                    pe.wait_ge(q["xs_ready"], j)
                for t in range(NT):
                    for k in range(2):
                        last = nc.tensor.transpose(PB[6][:, S * t + P * k:S * t + P * k + P], xcT[:, j % 2, k, P * t:P * t + P], ident)
                last.then_inc(q["xT_full"], 1)

            for j in range(8):
                gemm_a_fill(L1 + 9 + j, fills["x"] + j, hT)
                if j == 0:
                    values(23, False)
                if j == 1:
                    pe.wait_ge(q["dt_ready"], 1)
                    mm(PB[4][:, 0:NH], tri, dta[:, 1, :], start=True, stop=True)
                    mm(PB[4][:, 64:64 + NH], su, dta[:, 0, :], start=True, stop=True).then_inc(q["dta_full"], 1)
                if j >= 1:
                    x_transposes(j - 1)
            x_transposes(7)
            for s in range(2 * G):
                c, g = divmod(s, G)
                BT, CT = BCT[:, g, P * c:P * c + P], BCT[:, G + g, P * c:P * c + P]
                if s == 0:
                    pe.wait_ge(q["eac_done"], 2)
                    pe.wait_ge(q["silu_conv"], 24)
                    pe.wait_ge(q["cat_done"], 24)
                    fills_drained(pe, "x")
                if s >= 1:
                    pe.wait_ge(q["cbm_done"], s)
                if s >= 1 and s <= G:
                    pe.wait_ge(q["btok_done"], s)
                mm(PB[7][:, 0:P], BT, CT, start=True, stop=True).then_inc(q["cb_full"], 1)
                if c == 0:
                    pe.wait_ge(q["cbm_done"], s + 1)
                    nc.tensor.transpose(PB[7][:, 256:384], BT, ident).then_inc(q["bt_full"], 1)
                for half in range(2):
                    n = 2 * s + half
                    pe.wait_ge(q["l_ready"], n + 1)
                    if n >= 2:
                        pe.wait_ge(q["dec_done"], n - 1)
                    for h in range(4):
                        last = mm(PB[4 + n % 2][:, P * h:P * h + P], Lm[:, n % 2, h, :], tri, start=True, stop=True)
                    last.then_inc(q["seg_full"], 1)
                if c == 0:
                    pe.wait_ge(q["btok_done"], s + 1)
                    pe.wait_ge(q["xde_ready"], s + 1)
                    if s >= 1:
                        pe.wait_ge(q["st_done"], s)
                    mm(PB[6][:, :], btok[:, :], xde[:, :, :].rearrange("p h d -> p (h d)"), start=True, stop=True).then_inc(q["st_full"], 1)
                else:
                    pe.wait_ge(q["st_done"], G)
                    if s > G:
                        pe.wait_ge(q["yo_done"], 2 * (s - G))
                    mm(PB[6][:, :], CT, st[:, g, :], start=True, stop=True).then_inc(q["yo_full"], 1)
                pe.wait_ge(q["xdt_ready"], s + 1)
                if s >= 2:
                    pe.wait_ge(q["yy_done"], s - 1)
                for h in range(HPG):
                    n = 2 * s + h // 4
                    pe.wait_ge(q["m_ready"], n + 1)
                    last = mm(PB[2 + s % 2][:, PH * h:PH * h + PH], dec[:, n % 2, h % 4, :], xdt[:, h, :], start=True, stop=True)
                last.then_inc(q["yd_full"], 1)
            pe.wait_ge(q["yy_done"], 2 * G)
            for j in range(4):
                gemm_b(L1 + 17 + 2 * j, fills["z"] + 2 * j, 2, hT)
            transposed(R_Y, y, DI)
            pe.wait_ge(q["t_lo"], 28)
            for j in range(2):
                gemm_b(L1 + 25 + 6 * j, fills["out1"] + 2 * j, 6, cat)
            transposed(R_F1, xn, D)
            pe.wait_ge(q["tr_drained"], 32)
            for t in range(NT):
                for k in range(KD):
                    last = mm(PB[0][:, NE * t:NE * t + NE], hTf[:, k, P * t:P * t + P], pc[:, PC_RT + NE * k:PC_RT + NE * k + NE],
                              start=k == 0, stop=k == KD - 1)
            last.then_inc(q["lg_full"], 1)
            pe.wait_ge(q["top_done"], 1)
            ones, before_me = con[:, C_ONE:C_ONE + P], con[:, C_ST:C_ST + P]
            mm(PB[1][:, 0:NE], before_me, top[:, 0, :], start=True, stop=True)
            mm(PB[1][:, NE:2 * NE], ones, top[:, 0, :], start=True, stop=False)
            mm(PB[1][:, NE:2 * NE], before_me, top[:, 1, :], start=False, stop=True)
            mm(PB[1][:, 2 * NE:3 * NE], ones, top[:, 0, :], start=True, stop=False)
            mm(PB[1][:, 2 * NE:3 * NE], ones, top[:, 1, :], start=False, stop=True).then_inc(q["pos_full"], 1)

            def gather(job, i):
                src = (hn_hi, hn_lo)[i // 2]
                for k in range(4):
                    for t in range(NT):
                        last = mm(PB[GATHER_BANK[i]][:, P * k:P * k + P], src[:, t, P * (4 * (i % 2) + k):P * (4 * (i % 2) + k) + P], sel[:, t, :],
                                  start=t == 0, stop=t == NT - 1)
                last.then_inc(q["ga_full"], 1)

            pe.wait_ge(q["sel_ready"], 1)
            pe.wait_ge(q["hn_ready"], 3)
            pe.wait_ge(q["rt_chain"], 24)
            for i in range(4):
                if i == 3:
                    pe.wait_ge(q["ga_done"], 1)
                gather(0, i)
            pe.wait_ge(q["jobs_ready"], 1)
            last_job = pe.value_load(jobs_i[0:1, 0:1], min_val=NE - 1, max_val=NE - 1 + OVER)

            def scatter(job, i):
                t, n = divmod(i, 2)
                if i:
                    pe.wait_ge(q["sc_done"], 4 * job + i)
                else:
                    pe.wait_ge(q["ylo_done"], 2 * job + 2)
                    pe.wait_ge(q["selT_done"], job + 1)
                for k, part in enumerate((y_hi, y_lo)):
                    last = mm(PB[7][:, :], selT[:, t, :], part[:, 512 * n:512 * n + 512], start=k == 0, stop=k == 1)
                last.then_inc(q["sc_full"], 1)

            xg = (xg_hi, xg_lo)
            aT = (aT_hi, aT_lo)

            def expert(job, last_one):
                def rows(c, part):
                    bank = PB[2 * (c % 2) + part]
                    if c >= 2 and part == 0:
                        pe.wait_ge(q["e_act"], FCJ * job + c - 1)
                    m = job_unit(c, part)
                    if c == FCJ - 1:
                        split_ready(MOE + m, job)
                        w = parts(MOE + m, "a")
                        for k in range(KD):
                            last = mm3(bank[:, 0:256], cut(xg, ALL, k), cut(w, ALL, k), k == 0, k == KD - 1)
                        last.then_inc(q["units_used"], 1)
                    for kg in range(0 if c == FCJ - 1 else 2):
                        split_ready(MOE + m + kg, job)
                        w = parts(MOE + m + kg, "b")
                        for k in range(4):
                            last = mm3(bank[:, :], cut(xg, ALL, 4 * kg + k), cut(w, ALL, k), kg == 0 and k == 0, kg == 1 and k == 3)
                        last.then_inc(q["units_used"], 1)
                        yield kg

                def turn(c):
                    nk = 4 if c < FCJ - 1 else 2
                    pe.wait_ge(q["e_act"], FCJ * job + c + 1)
                    if c:
                        pe.wait_ge(q["e_tlo"], FCJ * job + c)
                    for k in range(nk):
                        last = nc.tensor.transpose(PB[4][:, P * k:P * k + P], actf[:, c % 2, P * k:P * k + P], ident)
                    last.then_inc(q["e_t"], 1)

                def down(c, n):
                    m = job_unit(c, 2) + n
                    split_ready(MOE + m, job)
                    if n == 0:
                        pe.wait_ge(q["e_tlo"], FCJ * job + c + 1)
                    w = parts(MOE + m, "b")
                    for k in range(4):
                        last = mm3(PB[5 + n][:, :], cut(aT, ALL, c % 2, k), cut(w, ALL, k), c == 0 and k == 0, False)
                    last.then_inc(q["units_used"], 1)

                pe.wait_ge(q["ga_done"], 4 * job + 4)
                for _ in rows(0, 0):
                    pass
                for _ in rows(0, 1):
                    pass
                for _ in rows(1, 0):
                    pass
                scatter(job, 0)
                turn(0)
                for kg in rows(1, 1):
                    if kg == 0:
                        scatter(job, 1)
                down(0, 0)
                scatter(job, 2)
                down(0, 1)
                for c in range(2, FCJ - 1):
                    for _ in rows(c, 0):
                        pass
                    if c == 2:
                        scatter(job, 3)
                    turn(c - 1)
                    for _ in rows(c, 1):
                        pass
                    down(c - 1, 0)
                    if c == 2:
                        pe.wait_ge(q["sc_done"], 4 * job + 4)
                        for t in range(NT):
                            last = nc.tensor.transpose(PB[7][:, P * t:P * t + P], sel[:, t, :].bitcast(F32), ident)
                        last.then_inc(q["selT_full"], 1)
                    down(c - 1, 1)
                c = FCJ - 1
                for _ in rows(c, 0):
                    pass
                turn(c - 1)
                for _ in rows(c, 1):
                    pass
                if not last_one:
                    pe.wait_ge(q["sel_ready"], job + 2)
                    pe.wait_ge(q["selT_done"], job + 2)
                    gather(job + 1, 0)
                    pe.wait_ge(q["e_act"], FCJ * job + c)
                    gather(job + 1, 1)
                down(c - 1, 0)
                turn(c)
                if not last_one:
                    gather(job + 1, 2)
                down(c - 1, 1)
                if not last_one:
                    pe.wait_ge(q["ga_done"], 4 * job + 5)
                    gather(job + 1, 3)
                m = UJ - 1
                split_ready(MOE + m, job)
                pe.wait_ge(q["e_tlo"], FCJ * job + c + 1)
                w = parts(MOE + m, "d")
                for n in range(2):
                    for k in range(2):
                        last = mm3(PB[5 + n][:, :], cut(aT, ALL, c % 2, k), cut(w, ALL, k, slice(512 * n, 512 * n + 512)), False, k == 1)
                last.then_inc(q["units_used"], 1)

            with pe.Fori(0, last_job) as job:
                expert(job, False)
            expert(last_job, True)
            for i in range(4):
                scatter(last_job + 1, i)


_NAMES = ["x", "mem", "w_mem_kv", "rel_bias", "swa_w_in", "swa_w_out", "ssm_w_in", "ssm_w_out",
          "ffn_w_gate", "ffn_w_up", "ffn_w_down", "moe_w_gate", "moe_w_up", "moe_w_down"]


def kernel(**inputs):
    import numpy as _np
    import concourse.bacc as _bacc
    from concourse.bass_utils import run_bass_kernel_spmd as _run

    i = {k: _np.ascontiguousarray(v) for k, v in inputs.items()}

    def tiles(v):
        return v.reshape(-1, P).T

    arrays = {n: i[n] for n in _NAMES}
    arrays["pcol"] = _np.ascontiguousarray(_np.concatenate(
        [tiles(i[g][layer]) for g in ("g_mix", "g_ffn", "g_mem") for layer in range(2)]
        + [i["ssm_conv_w"][0].reshape(CW, 24, P).transpose(2, 1, 0).reshape(P, 24 * CW)]
        + [tiles(i["ssm_conv_b"][0]), tiles(i["ssm_g_norm"][0])]
        + [i["moe_w_router"][0].reshape(KD, P, NE).transpose(1, 0, 2).reshape(P, KD * NE)], axis=1))
    arrays["prow"] = _np.ascontiguousarray(_np.concatenate(
        [i["swa_sinks"][0], i["ssm_dt_bias"][0], i["ssm_A_log"][0], i["ssm_D"][0]])[None, :])
    arrays["g_final"] = i["g_final"][None, :]
    arrays["g_ffn"] = i["g_ffn"]
    arrays["const"] = constants()
    arrays["bucket"] = bucket_rows()
    nc = _bacc.Bacc("TRN2", target_bir_lowering=False, num_devices=1)
    aps = {n: nc.dram_tensor(f"in_{n}", v.shape, F32, kind="ExternalInput").ap() for n, v in arrays.items()}
    out = nc.dram_tensor("out_0", (1, S, D), F32, kind="ExternalOutput").ap()
    trunk(nc, aps, out)
    r = _run(nc, [{f"in_{n}": v for n, v in arrays.items()}], core_ids=[0])
    return r.results[0]["out_0"]
```
